# Optimizing a Trainium2 kernel written in Bass

```python
import jax, jax.numpy as jnp
from jax import lax
import numpy as np
import math

D_MODEL = 1024
BATCH = 1
SEQ = 512
DEPTH = 1

GRID_W = 64
CTX_LEN = 256
HEAD_DIM = 64
ATTN_Q_HEADS = 8
ATTN_KV_HEADS = 2
ATTN_GROUP = ATTN_Q_HEADS // ATTN_KV_HEADS
WINDOW = 128
ATTN_BLOCK = 128
ROPE_BASE = 10000.0
DN_HEADS = 8
DN_HEAD_DIM = 64
CONV_W = 3
CHUNK = 64
N_DIR = 2
D_FF = 4 * D_MODEL
EPS = 1e-6
NEG_INF = -1e30

ATTN_WIDTH = ATTN_Q_HEADS * HEAD_DIM
KV_WIDTH = ATTN_KV_HEADS * HEAD_DIM
DN_WIDTH = DN_HEADS * DN_HEAD_DIM
IN_SPLITS = (ATTN_WIDTH, KV_WIDTH, KV_WIDTH, DN_WIDTH, DN_WIDTH, DN_WIDTH, DN_WIDTH,
             N_DIR * DN_HEADS, N_DIR * DN_HEADS, D_MODEL, D_MODEL)
IN_WIDTH = 4 * DN_WIDTH + ATTN_WIDTH + 2 * KV_WIDTH + 2 * N_DIR * DN_HEADS + 2 * D_MODEL


def rms_norm(x, g):
    xf = x.astype(jnp.float32)
    return xf * lax.rsqrt(jnp.mean(xf * xf, axis=-1, keepdims=True) + EPS) * g.astype(jnp.float32)

def l2_normalize(x):
    return x * lax.rsqrt(jnp.sum(x * x, axis=-1, keepdims=True) + EPS)

def split_cols(p):
    offsets = [int(o) for o in np.cumsum(IN_SPLITS)[:-1]]
    return jnp.split(p, offsets, axis=-1)

def axial_rope(x, row, col):
    half = HEAD_DIM // 2
    n_freq = half // 2
    freqs = ROPE_BASE ** (-jnp.arange(n_freq, dtype=jnp.float32) / n_freq)

    def rot(xh, pos):
        ang = pos.astype(jnp.float32)[:, None] * freqs
        cos = jnp.cos(ang)[None, :, None, :]
        sin = jnp.sin(ang)[None, :, None, :]
        x1, x2 = xh[..., :n_freq], xh[..., n_freq:]
        return jnp.concatenate([x1 * cos - x2 * sin, x1 * sin + x2 * cos], axis=-1)

    return jnp.concatenate([rot(x[..., :half], row), rot(x[..., half:], col)], axis=-1)

def centred_short_conv(x, w):
    pad = CONV_W // 2
    T = x.shape[1]
    xp = jnp.pad(x, ((0, 0), (pad, CONV_W - 1 - pad), (0, 0)))
    y = sum(xp[:, tap:tap + T] * w[tap] for tap in range(CONV_W))
    return jax.nn.silu(y)

def gated_delta_chunked(q, k, v, g_log, beta, s0):
    B, T, H, dk = q.shape
    n = T // CHUNK

    def chunks(a):
        return jnp.moveaxis(a.reshape((B, n, CHUNK, H) + a.shape[3:]), 3, 1)

    qc, kc, vc = chunks(q), chunks(k), chunks(v)
    gc, bc = chunks(g_log), chunks(beta)
    G = jnp.cumsum(gc, axis=-1)
    idx = jnp.arange(CHUNK)
    strict = idx[:, None] > idx[None, :]
    incl = idx[:, None] >= idx[None, :]
    diff = G[..., :, None] - G[..., None, :]
    dec_strict = jnp.where(strict, jnp.exp(jnp.where(strict, diff, 0.0)), 0.0)
    dec_incl = jnp.where(incl, jnp.exp(jnp.where(incl, diff, 0.0)), 0.0)
    kk = jnp.einsum('bhnid,bhnjd->bhnij', kc, kc)
    t_mat = jnp.eye(CHUNK, dtype=jnp.float32) + bc[..., :, None] * dec_strict * kk
    eG = jnp.exp(G)
    w_mat = lax.linalg.triangular_solve(t_mat, (bc * eG)[..., None] * kc, left_side=True, lower=True,
                                        unit_diagonal=True)
    u_v = lax.linalg.triangular_solve(t_mat, bc[..., None] * vc, left_side=True, lower=True,
                                      unit_diagonal=True)
    intra = dec_incl * jnp.einsum('bhnid,bhnjd->bhnij', qc, kc)
    q_dec = eG[..., None] * qc
    g_last = G[..., -1]
    k_tail = jnp.exp(g_last[..., None] - G)[..., None] * kc

    def step(S, xs):
        w_c, uv_c, qd_c, intra_c, kt_c, gl_c = xs
        u = uv_c - jnp.einsum('bhck,bhkv->bhcv', w_c, S)
        o = jnp.einsum('bhck,bhkv->bhcv', qd_c, S) + jnp.einsum('bhij,bhjv->bhiv', intra_c, u)
        S = jnp.exp(gl_c)[..., None, None] * S + jnp.einsum('bhck,bhcv->bhkv', kt_c, u)
        return S, o

    xs = tuple(jnp.moveaxis(a, 2, 0) for a in (w_mat, u_v, q_dec, intra, k_tail, g_last))
    s_final, o = lax.scan(step, s0, xs)
    o = jnp.transpose(o, (1, 0, 3, 2, 4)).reshape(B, T, H, v.shape[-1])
    return o, s_final

def bidir_delta(q, k, v, g, beta, s0_f, s0_b):
    o_f, s_f = gated_delta_chunked(q, k, v, g[:, :, 0], beta[:, :, 0], s0_f)
    flip = lambda a: jnp.flip(a, axis=1)
    o_b, s_b = gated_delta_chunked(flip(q), flip(k), flip(v), flip(g[:, :, 1]), flip(beta[:, :, 1]), s0_b)
    return o_f + flip(o_b), s_f, s_b

def window_ctx_attention(q, k, v, k_ctx, v_ctx, sink):
    B, S = q.shape[:2]
    L = k_ctx.shape[1]
    nb = S // ATTN_BLOCK
    qb = q.reshape(B, nb, ATTN_BLOCK, ATTN_KV_HEADS, ATTN_GROUP, HEAD_DIM)

    def band(a):
        ap = jnp.pad(a, ((0, 0), (ATTN_BLOCK, ATTN_BLOCK), (0, 0), (0, 0)))
        ap = ap.reshape(B, nb + 2, ATTN_BLOCK, ATTN_KV_HEADS, HEAD_DIM)
        return jnp.concatenate([ap[:, :-2], ap[:, 1:-1], ap[:, 2:]], axis=2)

    kb, vb = band(k), band(v)
    blk = jnp.arange(nb)[:, None, None]
    qpos = blk * ATTN_BLOCK + jnp.arange(ATTN_BLOCK)[None, :, None]
    kpos = (blk - 1) * ATTN_BLOCK + jnp.arange(3 * ATTN_BLOCK)[None, None, :]
    valid = (jnp.abs(qpos - kpos) <= WINDOW) & (kpos >= 0) & (kpos < S)
    scale = HEAD_DIM ** -0.5
    s_loc = jnp.einsum('bnqgrd,bnkgd->bngrqk', qb, kb) * scale
    s_loc = jnp.where(valid[None, :, None, None], s_loc, NEG_INF)
    s_ctx = jnp.einsum('bnqgrd,bkgd->bngrqk', qb, k_ctx) * scale
    s_sink = jnp.broadcast_to(sink.reshape(ATTN_KV_HEADS, ATTN_GROUP)[None, None, :, :, None, None],
                              s_loc.shape[:-1] + (1,))
    p = jax.nn.softmax(jnp.concatenate([s_loc, s_ctx, s_sink], axis=-1).astype(jnp.float32), axis=-1)
    n_loc = 3 * ATTN_BLOCK
    o = (jnp.einsum('bngrqk,bnkgd->bnqgrd', p[..., :n_loc], vb)
         + jnp.einsum('bngrqk,bkgd->bnqgrd', p[..., n_loc:n_loc + L], v_ctx))
    return o.reshape(B, S, ATTN_WIDTH)

def ctx_self_attention(q, k, v, sink):
    B, L = q.shape[:2]
    qg = q.reshape(B, L, ATTN_KV_HEADS, ATTN_GROUP, HEAD_DIM)
    s = jnp.einsum('bqgrd,bkgd->bgrqk', qg, k) * HEAD_DIM ** -0.5
    s_sink = jnp.broadcast_to(sink.reshape(ATTN_KV_HEADS, ATTN_GROUP)[None, :, :, None, None], s.shape[:-1] + (1,))
    p = jax.nn.softmax(jnp.concatenate([s, s_sink], axis=-1).astype(jnp.float32), axis=-1)
    o = jnp.einsum('bgrqk,bkgd->bqgrd', p[..., :L], v)
    return o.reshape(B, L, ATTN_WIDTH)

def trunk_layer(x, ctx, c, c_ctx, w_ada, b_ada, g_norm1, w_in, q_norm_g, k_norm_g, attn_sink, conv_w,
                a_log, dt_bias, dn_norm_g, w_br_attn, w_br_dn, w_out, g_norm2, w_mlp1, w_mlp2, update_ctx):
    B, S = x.shape[:2]
    L = ctx.shape[1]
    rows = S // GRID_W
    row = jnp.broadcast_to(jnp.arange(rows)[:, None], (rows, GRID_W)).reshape(-1)
    col = jnp.broadcast_to(jnp.arange(GRID_W)[None, :], (rows, GRID_W)).reshape(-1)

    mod = jax.nn.silu(c.astype(jnp.float32)) @ w_ada + b_ada
    mod_c = jax.nn.silu(c_ctx.astype(jnp.float32)) @ w_ada + b_ada
    sh1, sc1, gt1, sh2, sc2, gt2 = [m[:, None] for m in jnp.split(mod, 6, axis=-1)]
    csh1, csc1, cgt1, csh2, csc2, cgt2 = jnp.split(mod_c, 6, axis=-1)

    h = rms_norm(x, g_norm1) * (1.0 + sc1) + sh1
    hc = rms_norm(ctx, g_norm1) * (1.0 + csc1) + csh1
    aq, ak, av, dq, dk, dv, dz, da, db, ga, gd = split_cols(h @ w_in)
    caq, cak, cav, cdq, cdk, cdv, cdz, cda, cdb, cga, cgd = split_cols(hc @ w_in)

    def heads(a, n_heads):
        return a.reshape(a.shape[0], a.shape[1], n_heads, HEAD_DIM)

    q_a = axial_rope(rms_norm(heads(aq, ATTN_Q_HEADS), q_norm_g), row, col)
    k_a = axial_rope(rms_norm(heads(ak, ATTN_KV_HEADS), k_norm_g), row, col)
    v_a = heads(av, ATTN_KV_HEADS)
    k_ac = rms_norm(heads(cak, ATTN_KV_HEADS), k_norm_g)
    v_ac = heads(cav, ATTN_KV_HEADS)
    y_attn = window_ctx_attention(q_a, k_a, v_a, k_ac, v_ac, attn_sink)

    def dn_inputs(pq, pk, pv, pa, pb):
        qkv = centred_short_conv(jnp.concatenate([pq, pk, pv], axis=-1), conv_w)
        q_d, k_d, v_d = jnp.split(qkv, 3, axis=-1)
        q_d = l2_normalize(heads(q_d, DN_HEADS)) * DN_HEAD_DIM ** -0.5
        k_d = l2_normalize(heads(k_d, DN_HEADS))
        v_d = heads(v_d, DN_HEADS)
        T = pq.shape[1]
        beta = jax.nn.sigmoid(pb.reshape(pb.shape[0], T, N_DIR, DN_HEADS))
        g = -jnp.exp(a_log) * jax.nn.softplus(pa.reshape(pa.shape[0], T, N_DIR, DN_HEADS) + dt_bias)
        return q_d, k_d, v_d, g, beta

    s_zero = jnp.zeros((B, DN_HEADS, DN_HEAD_DIM, DN_HEAD_DIM), jnp.float32)
    o_dc, s_cf, s_cb = bidir_delta(*dn_inputs(cdq, cdk, cdv, cda, cdb), s_zero, s_zero)
    o_dl, _, _ = bidir_delta(*dn_inputs(dq, dk, dv, da, db), s_cf, s_cb)

    def merge(y_a, o_d, z, gate_a, gate_d):
        y_d = (rms_norm(o_d, dn_norm_g) * jax.nn.silu(heads(z, DN_HEADS))).reshape(z.shape)
        y = jax.nn.sigmoid(gate_a) * (y_a @ w_br_attn) + jax.nn.sigmoid(gate_d) * (y_d @ w_br_dn)
        return y @ w_out

    def mlp(s, shift, scale_m):
        hm = rms_norm(s, g_norm2) * (1.0 + scale_m) + shift
        return jnp.square(jax.nn.relu(hm @ w_mlp1)) @ w_mlp2

    x_new = x.astype(jnp.float32) + gt1 * merge(y_attn, o_dl, dz, ga, gd)
    x_new = x_new + gt2 * mlp(x_new, sh2, sc2)

    if update_ctx:
        q_ac = rms_norm(heads(caq, ATTN_Q_HEADS), q_norm_g)
        y_attn_c = ctx_self_attention(q_ac, k_ac, v_ac, attn_sink)
        ctx = ctx.astype(jnp.float32) + cgt1 * merge(y_attn_c, o_dc, cdz, cga, cgd)
        ctx = ctx + cgt2 * mlp(ctx, csh2, csc2)
    return x_new, ctx

def first_inputs(seed: int = 0) -> dict:
    key = jax.random.key(seed)
    ks = jax.random.split(key, 24)
    f32 = jnp.float32
    nrm = lambda k, shape, s: jax.random.normal(k, shape, f32) * s
    dt = jnp.exp(jax.random.uniform(ks[12], (DEPTH, N_DIR, DN_HEADS), f32, np.log(1e-3), np.log(1e-1)))
    return {
        "x": nrm(ks[0], (BATCH, SEQ, D_MODEL), 1.0),
        "c": nrm(ks[1], (BATCH, D_MODEL), 1.0),
        "ctx": nrm(ks[2], (BATCH, CTX_LEN, D_MODEL), 1.0),
        "c_ctx": nrm(ks[3], (D_MODEL,), 1.0),
        "w_ada": nrm(ks[4], (DEPTH, D_MODEL, 6 * D_MODEL), 0.5 * D_MODEL ** -0.5),
        "b_ada": nrm(ks[5], (DEPTH, 6 * D_MODEL), 0.02),
        "g_norm1": 1.0 + nrm(ks[6], (DEPTH, D_MODEL), 0.1),
        "w_in": nrm(ks[7], (DEPTH, D_MODEL, IN_WIDTH), D_MODEL ** -0.5),
        "q_norm_g": 1.0 + nrm(ks[8], (DEPTH, HEAD_DIM), 0.1),
        "k_norm_g": 1.0 + nrm(ks[9], (DEPTH, HEAD_DIM), 0.1),
        "attn_sink": nrm(ks[10], (DEPTH, ATTN_Q_HEADS), 0.5),
        "conv_w": nrm(ks[11], (DEPTH, CONV_W, 3 * DN_WIDTH), CONV_W ** -0.5),
        "a_log": jnp.log(jax.random.uniform(ks[13], (DEPTH, N_DIR, DN_HEADS), f32, 1.0, 16.0)),
        "dt_bias": dt + jnp.log(-jnp.expm1(-dt)),
        "dn_norm_g": 1.0 + nrm(ks[14], (DEPTH, DN_HEAD_DIM), 0.1),
        "w_br_attn": nrm(ks[15], (DEPTH, ATTN_WIDTH, D_MODEL), ATTN_WIDTH ** -0.5),
        "w_br_dn": nrm(ks[16], (DEPTH, DN_WIDTH, D_MODEL), DN_WIDTH ** -0.5),
        "w_out": nrm(ks[17], (DEPTH, D_MODEL, D_MODEL), D_MODEL ** -0.5),
        "g_norm2": 1.0 + nrm(ks[18], (DEPTH, D_MODEL), 0.1),
        "w_mlp1": nrm(ks[19], (DEPTH, D_MODEL, D_FF), D_MODEL ** -0.5),
        "w_mlp2": nrm(ks[20], (DEPTH, D_FF, D_MODEL), D_FF ** -0.5),
    }

def first_block(x, c, ctx, c_ctx, w_ada, b_ada, g_norm1, w_in, q_norm_g, k_norm_g, attn_sink, conv_w,
              a_log, dt_bias, dn_norm_g, w_br_attn, w_br_dn, w_out, g_norm2, w_mlp1, w_mlp2):
    out_dtype = x.dtype
    for layer in range(DEPTH):
        x, ctx = trunk_layer(x, ctx, c, c_ctx, w_ada[layer], b_ada[layer], g_norm1[layer], w_in[layer],
                             q_norm_g[layer], k_norm_g[layer], attn_sink[layer], conv_w[layer],
                             a_log[layer], dt_bias[layer], dn_norm_g[layer], w_br_attn[layer],
                             w_br_dn[layer], w_out[layer], g_norm2[layer], w_mlp1[layer], w_mlp2[layer],
                             update_ctx=layer < DEPTH - 1)
    return x.astype(out_dtype)


DEPTH_2 = 2

POOL_WIDTH = 512
POOL_WINDOWS = (2, 4, 8, 16)
POOL_GROUPS = len(POOL_WINDOWS)
POOL_GC = POOL_WIDTH // POOL_GROUPS
N_HEADS = 4
V_DIM = 2 * HEAD_DIM
QK_WIDTH = N_HEADS * 2 * HEAD_DIM
ATTN_WIDTH_2 = N_HEADS * V_DIM
MIX_WIDTH = POOL_WIDTH + ATTN_WIDTH_2
IN_WIDTH_2 = POOL_WIDTH + 2 * QK_WIDTH + ATTN_WIDTH_2
ROT_AXIS = HEAD_DIM // 2
D_FF_2 = 4 * D_MODEL
Q_BLOCK = 128
N_ADA = 6


def rms_norm_2(x, g):
    xf = x.astype(jnp.float32)
    y = xf * lax.rsqrt(jnp.mean(xf * xf, axis=-1, keepdims=True) + EPS)
    return (y * g.astype(jnp.float32)).astype(x.dtype)

def modulate(h, shift, scale):
    return h * (1 + scale) + shift

def ada_params(cvec, w_ada, b_ada):
    return jnp.split(jax.nn.silu(cvec) @ w_ada + b_ada, N_ADA, axis=-1)

def axial_rope_2(n, dtype):
    rows = n // GRID_W
    row = jnp.repeat(jnp.arange(rows), GRID_W).astype(jnp.float32)
    col = jnp.tile(jnp.arange(GRID_W), rows).astype(jnp.float32)
    inv = ROPE_BASE ** (-jnp.arange(0, ROT_AXIS, 2, dtype=jnp.float32) / ROT_AXIS)
    ang = jnp.concatenate([row[:, None] * inv, col[:, None] * inv], axis=-1)
    return jnp.cos(ang).astype(dtype), jnp.sin(ang).astype(dtype)

def apply_rope(x, cos, sin):
    x1, x2 = x[..., :HEAD_DIM // 2], x[..., HEAD_DIM // 2:]
    return jnp.concatenate([x1 * cos - x2 * sin, x1 * sin + x2 * cos], axis=-1)

def centred_mean(x, w):
    b, n, ch = x.shape
    xf = x.astype(jnp.float32)
    cs = jnp.concatenate([jnp.zeros((b, 1, ch), jnp.float32), jnp.cumsum(xf, axis=1)], axis=1)
    t = jnp.arange(n)
    lo = jnp.clip(t - w // 2, 0, n)
    hi = jnp.clip(t + w - w // 2, 0, n)
    s = cs[:, hi] - cs[:, lo]
    cnt = (hi - lo).astype(jnp.float32)
    return (s / cnt[None, :, None]).astype(x.dtype)

def pool_mixer(u, w_pool, s_pool):
    b, n, _ = u.shape
    groups = jnp.split(u, POOL_GROUPS, axis=-1)
    y = jnp.stack([centred_mean(g, w) - g for g, w in zip(groups, POOL_WINDOWS)], axis=2)
    y = jnp.einsum('bngc,gcd->bngd', y, w_pool).reshape(b, n, POOL_WIDTH)
    return y * s_pool

def split_heads(z):
    b, n, _ = z.shape
    u, q, k, v = jnp.split(z, [POOL_WIDTH, POOL_WIDTH + QK_WIDTH, POOL_WIDTH + 2 * QK_WIDTH], axis=-1)
    q = q.reshape(b, n, 2 * N_HEADS, HEAD_DIM).transpose(0, 2, 1, 3)
    k = k.reshape(b, n, 2 * N_HEADS, HEAD_DIM).transpose(0, 2, 1, 3)
    v = v.reshape(b, n, N_HEADS, V_DIM).transpose(0, 2, 1, 3)
    return u, q, k, v

def diff_attn(q, k, v, lam):
    b, _, nq, _ = q.shape
    nk = k.shape[2]
    s = jnp.einsum('bhqd,bhkd->bhqk', q, k).astype(jnp.float32) * (HEAD_DIM ** -0.5)
    a = jax.nn.softmax(s, axis=-1).reshape(b, N_HEADS, 2, nq, nk)
    w = a[:, :, 0] - lam * a[:, :, 1]
    return jnp.einsum('bhqk,bhkd->bhqd', w.astype(v.dtype), v)

def diff_attn_blocks(q, k, v, lam):
    b, hh, n, d = q.shape
    nb = n // Q_BLOCK
    qb = q.reshape(b, hh, nb, Q_BLOCK, d).transpose(2, 0, 1, 3, 4)
    o = lax.map(lambda qblk: diff_attn(qblk, k, v, lam), qb)
    return o.transpose(1, 2, 0, 3, 4).reshape(b, N_HEADS, n, V_DIM)

def head_out(o, g_sub, lam_init):
    o = rms_norm_2(o, g_sub) * (1.0 - lam_init)
    b, h, n, d = o.shape
    return o.transpose(0, 2, 1, 3).reshape(b, n, h * d)

def sq_relu_mlp(h, w1, w2):
    return jnp.square(jax.nn.relu(h @ w1)) @ w2

def second_inputs(seed: int = 0) -> dict:
    key = jax.random.key(seed)
    ks = jax.random.split(key, 24)
    f = jnp.float32
    nrm = lambda k, shape, s: jax.random.normal(k, shape, f) * s
    L = DEPTH_2
    return {
        "x": nrm(ks[0], (BATCH, SEQ, D_MODEL), 1.0),
        "c": nrm(ks[1], (BATCH, D_MODEL), 1.0),
        "ctx": nrm(ks[2], (BATCH, CTX_LEN, D_MODEL), 1.0),
        "c_ctx": nrm(ks[3], (D_MODEL,), 1.0),
        "w_ada": nrm(ks[4], (L, D_MODEL, N_ADA * D_MODEL), 0.02),
        "b_ada": nrm(ks[5], (L, N_ADA * D_MODEL), 0.01),
        "g_mix": 1.0 + nrm(ks[6], (L, D_MODEL), 0.02),
        "g_mlp": 1.0 + nrm(ks[7], (L, D_MODEL), 0.02),
        "w_in": nrm(ks[8], (L, D_MODEL, IN_WIDTH_2), D_MODEL ** -0.5),
        "w_pool": nrm(ks[9], (L, POOL_GROUPS, POOL_GC, POOL_GC), POOL_GC ** -0.5),
        "s_pool": 1.0 + nrm(ks[10], (L, POOL_WIDTH), 0.1),
        "lam_q1": nrm(ks[11], (L, HEAD_DIM), 0.1),
        "lam_k1": nrm(ks[12], (L, HEAD_DIM), 0.1),
        "lam_q2": nrm(ks[13], (L, HEAD_DIM), 0.1),
        "lam_k2": nrm(ks[14], (L, HEAD_DIM), 0.1),
        "g_subln": 1.0 + nrm(ks[15], (L, V_DIM), 0.02),
        "w_out": nrm(ks[16], (L, MIX_WIDTH, D_MODEL), MIX_WIDTH ** -0.5),
        "w_mlp1": nrm(ks[17], (L, D_MODEL, D_FF_2), D_MODEL ** -0.5),
        "w_mlp2": nrm(ks[18], (L, D_FF_2, D_MODEL), D_FF_2 ** -0.5),
        "g_final": 1.0 + nrm(ks[19], (D_MODEL,), 0.02),
    }

def second_block(x, c, ctx, c_ctx, w_ada, b_ada, g_mix, g_mlp, w_in, w_pool, s_pool,
              lam_q1, lam_k1, lam_q2, lam_k2, g_subln, w_out, w_mlp1, w_mlp2, g_final):
    n = x.shape[1]
    cos, sin = axial_rope_2(n, x.dtype)
    c_lat = c[:, None, :]
    c_cx = c_ctx[None, None, :]
    for l in range(DEPTH_2):
        last = l == DEPTH_2 - 1
        sa, ca, ga, sm, cm, gm = ada_params(c_lat, w_ada[l], b_ada[l])
        sa_c, ca_c, ga_c, sm_c, cm_c, gm_c = ada_params(c_cx, w_ada[l], b_ada[l])
        lam_init = 0.8 - 0.6 * math.exp(-0.3 * l)
        lam = (jnp.exp(jnp.sum(lam_q1[l].astype(jnp.float32) * lam_k1[l].astype(jnp.float32)))
               - jnp.exp(jnp.sum(lam_q2[l].astype(jnp.float32) * lam_k2[l].astype(jnp.float32)))
               + lam_init)

        h = modulate(rms_norm_2(x, g_mix[l]), sa, ca)
        hc = modulate(rms_norm_2(ctx, g_mix[l]), sa_c, ca_c)
        u, q, k, v = split_heads(h @ w_in[l])
        uc, qc, kc, vc = split_heads(hc @ w_in[l])
        q = apply_rope(q, cos, sin)
        k = apply_rope(k, cos, sin)
        k_all = jnp.concatenate([kc, k], axis=2)
        v_all = jnp.concatenate([vc, v], axis=2)
        o_att = diff_attn_blocks(q, k_all, v_all, lam)
        mix = jnp.concatenate([pool_mixer(u, w_pool[l], s_pool[l]),
                               head_out(o_att, g_subln[l], lam_init)], axis=-1)
        x = x + ga * (mix @ w_out[l])

        x = x + gm * sq_relu_mlp(modulate(rms_norm_2(x, g_mlp[l]), sm, cm), w_mlp1[l], w_mlp2[l])

        if not last:
            o_c = diff_attn(qc, kc, vc, lam)
            mix_c = jnp.concatenate([pool_mixer(uc, w_pool[l], s_pool[l]),
                                     head_out(o_c, g_subln[l], lam_init)], axis=-1)
            ctx = ctx + ga_c * (mix_c @ w_out[l])
            ctx = ctx + gm_c * sq_relu_mlp(modulate(rms_norm_2(ctx, g_mlp[l]), sm_c, cm_c),
                                           w_mlp1[l], w_mlp2[l])
    return rms_norm_2(x, g_final)


def setup_inputs(seed=0):
    out = dict(first_inputs(seed))
    for name, value in second_inputs(seed + 1).items():
        if name != "x":
            out[name + "_2"] = value
    return out


def reference(
    x, c, ctx, c_ctx, w_ada, b_ada, g_norm1, w_in, q_norm_g, k_norm_g, attn_sink, conv_w, a_log,
    dt_bias, dn_norm_g, w_br_attn, w_br_dn, w_out, g_norm2, w_mlp1, w_mlp2, c_2, ctx_2, c_ctx_2,
    w_ada_2, b_ada_2, g_mix_2, g_mlp_2, w_in_2, w_pool_2, s_pool_2, lam_q1_2, lam_k1_2,
    lam_q2_2, lam_k2_2, g_subln_2, w_out_2, w_mlp1_2, w_mlp2_2, g_final_2,
):
    x = first_block(
        x, c, ctx, c_ctx, w_ada, b_ada, g_norm1, w_in, q_norm_g, k_norm_g, attn_sink, conv_w,
        a_log, dt_bias, dn_norm_g, w_br_attn, w_br_dn, w_out, g_norm2, w_mlp1, w_mlp2,
    )
    return second_block(
        x, c_2, ctx_2, c_ctx_2, w_ada_2, b_ada_2, g_mix_2, g_mlp_2, w_in_2, w_pool_2, s_pool_2,
        lam_q1_2, lam_k1_2, lam_q2_2, lam_k2_2, g_subln_2, w_out_2, w_mlp1_2, w_mlp2_2,
        g_final_2,
    )


_drawn_inputs = setup_inputs


def setup_inputs(seed=0):
    import zlib

    import numpy as np

    out = dict(_drawn_inputs(seed))
    spreads = {}
    factors = {'ctx': 3.89,
     'g_norm1': 2.672,
     'q_norm_g': 8.0,
     'k_norm_g': 8.0,
     'attn_sink': 8.0,
     'dn_norm_g': 5.29,
     'g_mix_2': 7.854,
     'g_mlp_2': 4.124,
     'lam_q2_2': 5.594,
     'g_subln_2': 22.165}
    for name, (base, spread) in spreads.items():
        noise = np.random.default_rng([zlib.crc32(name.encode()), seed]).standard_normal(out[name].shape)
        drawn = base * np.exp(spread * noise) if base else spread * noise
        out[name] = __import__('jax').numpy.asarray(drawn.astype(out[name].dtype))
    for name, factor in factors.items():
        out[name] = (out[name] * factor).astype(out[name].dtype)
    return out
```

```python
from contextlib import ExitStack

import numpy as np

import concourse.bass as bass
from concourse import mybir

F32 = mybir.dt.float32
F32R = mybir.dt.float32r
ALU = mybir.AluOpType
ACT = mybir.ActivationFunctionType
AXX = mybir.AxisListType.X

P = 128
KT = 8
T = 512
TC = 256
EPS = 1e-6
SET_EXP_LN = 6
SET_SIGMOID = 2
NEG = -1e30

CONSTS = (("ident", 128), ("bd", 128), ("perm1", 128), ("trif", 128), ("trib", 128),
          ("mprev", 128), ("mnext", 128), ("i64", 64), ("mstrict", 128), ("mincl", 128), ("lvl", 6 * 64),
          ("sel", 32))
CONSTS2 = (("perm2", 128), ("edge", 64))
CW = sum(w for _, w in CONSTS)
CW2 = sum(w for _, w in CONSTS2)
PAR1 = (("c", 16), ("bada", 48), ("gn1", 8), ("gn2", 8), ("qg", 1), ("kg", 1), ("sink", 8), ("convw", 36),
        ("alog", 1), ("dtb", 1), ("dng", 1))
PAR2 = (("c", 16), ("bada", 48), ("gmix", 8), ("gmlp", 8), ("spool", 4), ("gsub", 1), ("lam", 4), ("gfin", 8))
PW1 = sum(w for _, w in PAR1)
PW2 = sum(w for _, w in PAR2)


def offsets(fields):
    at, out = 0, {}
    for n, w in fields:
        out[n] = (at, w)
        at += w
    return out


class Engine:

    def __init__(self, name, sem, chained=True):
        self.name, self.sem, self.count, self.ops, self.seen = name, sem, 0, [], {}
        self.chained = chained

    def wait(self, *tokens):
        for t in tokens:
            if t is None:
                continue
            sem, value, key = t
            if self.seen.get(key, 0) < value:
                self.seen[key] = value
                self.ops.append(lambda e, s=sem, v=value: e.wait_ge(s, v))

    def __call__(self, fn, *after):
        self.wait(*after)
        if self.chained and self.count:
            self.wait(self.last())
        self.count += 1
        self.ops.append(lambda e: fn(e).then_inc(self.sem, 1))
        return (self.sem, self.count, self.name)

    def silent(self, fn, *after):
        self.wait(*after)
        self.ops.append(lambda e: fn(e))

    def last(self):
        return (self.sem, self.count, self.name)


class Dma:

    def __init__(self, sem, key):
        self.sem, self.key, self.n = sem, key, 0

    def start(self, q, out, in_, *after):
        q.wait(*after)
        self.n += 16
        q.ops.append(lambda e: e.dma_start(out, in_).then_inc(self.sem, 16))
        return (self.sem, self.n, self.key)


def build(nc, I, out):
    ctx = ExitStack()
    with ctx:
        def sem(name):
            return ctx.enter_context(nc.semaphore(name))

        pe = Engine("pe", sem("s_pe"), chained=False)
        dve = Engine("dve", sem("s_dve"))
        act = Engine("act", sem("s_act"))
        pool = Engine("pool", sem("s_pool"))
        sp = Engine("sp", sem("s_sp"))
        engines = (pe, dve, act, pool)

        def sb(name, shape, dt=F32, stack=ctx):
            return stack.enter_context(nc.sbuf_tensor(name, shape, dt))

        RAWN, WSN = 3, 3
        raw = sb("raw", [P, RAWN, 4096])
        ws = sb("ws", [P, WSN, 2, 1024], F32R)
        hh = sb("hh", [P, 2, KT, T], F32R)
        xT = sb("xT", [P, KT, T])
        cst = sb("cst", [P, CW])
        mods = sb("mods", [P, 3, 48, 2])
        par1 = sb("par1", [P, PW1])
        par2 = sb("par2", [P, 2, PW2])
        mvec = sb("mvec", [P, 64])
        ones = sb("ones", [P, P])
        rs = sb("rs", [P, T])
        sq = sb("sq", [P, 2, T])
        mi = sb("mi", [P, 8])
        REST = 18432

        def region(names):
            st = ExitStack()
            got = [sb(n, s, dt, st) for n, s, dt in names]
            st.close()
            return got

        ar, = region([("ar", [P, REST], F32)])
        hc1, = region([("hc1", [P, 2, KT, TC], F32R)])
        gg, yy = region([("gg", [P, 2, KT, T], F32R), ("yy", [P, 2, KT, T], F32R)])
        ctx2, hc2, ar2 = region([("ctx2", [P, KT, TC], F32), ("hc2", [P, 2, KT, TC], F32R),
                                 ("ar2", [P, REST - 6144], F32)])
        _, _, g2, gc2 = region([("pad_a", [P, KT, TC], F32), ("pad_b", [P, 2, KT, TC], F32R),
                                ("g2", [P, 2, KT, T], F32R), ("gc2", [P, 2, KT, TC], F32R)])

        psum = [ctx.enter_context(nc.psum_tensor(f"ps{i}", [P, 1024], F32)) for i in range(4)]
        bank_free = [[] for _ in range(8)]
        bank_at = [0]

        rotating = [8]
        held = [False] * 8

        def bank():
            for _ in range(8):
                b = bank_at[0] % rotating[0]
                bank_at[0] = b + 1
                if not held[b]:
                    held[b] = True
                    return b, psum[b // 2][:, (b % 2) * 512:(b % 2) * 512 + 512], bank_free[b]
            raise ValueError("no bank is free")

        def bank2():
            for _ in range(8):
                b = (bank_at[0] + bank_at[0] % 2) % rotating[0]
                bank_at[0] = b + 2
                if not held[b] and not held[b + 1]:
                    held[b] = held[b + 1] = True
                    return b, psum[b // 2], bank_free[b] + bank_free[b + 1]
            raise ValueError("no pair of banks is free")

        def bank_held():
            b = 7 if held[6] else 6
            assert not held[b]
            held[b] = True
            return b, psum[3][:, (b - 6) * 512:(b - 6) * 512 + 512], bank_free[b]

        def release(b, *tokens):
            bank_free[b] = list(tokens)
            held[b] = False

        def release2(b, *tokens):
            bank_free[b] = bank_free[b + 1] = list(tokens)
            held[b] = held[b + 1] = False

        co, co2 = offsets(CONSTS), offsets(CONSTS2)

        def C(name):
            if name in co2:
                a, w = co2[name]
                a += CW - CW2
            else:
                a, w = co[name]
            return cst[:, a:a + w]

        d_small = [Dma(sem(f"d_small{i}"), f"d_small{i}") for i in range(8)]
        d_raw = [Dma(sem(f"d_raw{i}"), f"d_raw{i}") for i in range(RAWN)]
        t_cst = d_small[0].start(pool, cst[:, :], I["consts"])
        t_x = d_small[1].start(pool, xT[:, :, :], I["xT"])

        raw_free = [[] for _ in range(RAWN)]
        raw_order = list(range(RAWN))
        raw_busy = [False] * RAWN

        def place():
            k = next(k for k in raw_order if not raw_busy[k])
            raw_order.remove(k)
            raw_order.append(k)
            raw_busy[k] = True

            def done(*tokens):
                raw_free[k] = list(tokens)
                raw_busy[k] = False
            return k, done

        def load(src, w):
            k, done = place()
            t = d_raw[k].start(sp, raw[:, k, 0:w], src, *raw_free[k])
            return raw[:, k, 0:w], t, done

        def reserve():
            k, done = place()
            return raw[:, k, :], raw_free[k], done

        plan = []
        ready = []
        ws_n = [0]
        ws_free = [None] * WSN
        cur = [None]

        def split_next():
            if cur[0] is None:
                src, kt, cols, pk, pc = plan.pop(0)
                w, t_w, done = load(src, kt * cols)
                wv = w.rearrange("p (k c) -> p k c", k=kt)
                pieces = [wv[:, k:k + pk, c:c + pc] for k in range(0, kt, pk) for c in range(0, cols, pc)]
                cur[0] = [pieces, t_w, done, pk, pc]
            pieces, t_w, done, pk, pc = cur[0]
            w = pieces.pop(0)
            s = ws_n[0] % WSN
            ws_n[0] += 1
            hi = ws[:, s, 0, 0:pk * pc].rearrange("p (k c) -> p k c", k=pk)
            lo = ws[:, s, 1, 0:pk * pc].rearrange("p (k c) -> p k c", k=pk)
            t_hi = act(lambda e: e.activation(hi, w, ACT.Copy), t_w, ws_free[s])
            t_lo = dve(lambda e: e.tensor_tensor(lo, w, hi.bitcast(F32), ALU.subtract), t_hi, t_w, ws_free[s])
            if not pieces:
                done(t_hi, t_lo)
                cur[0] = None
            ready.append((s, hi, lo, t_hi, t_lo))

        def coming(*blocks, kt=KT, cols=512, pk=KT, pc=128):
            plan.extend((src, kt, cols, pk, pc) for src in blocks)

        def piece():
            while len(ready) < WSN and (cur[0] is not None or plan):
                split_next()
            return ready.pop(0)

        pending = []

        def later(stages):
            for g in list(pending):
                if next(g, "end") == "end":
                    pending.remove(g)
            if stages is not None:
                pending.append(stages)

        def flush():
            while pending:
                later(None)

        def mm(o, l, r, start, stop, *after):
            return pe(lambda e: e.matmul(o, l, r, start=start, stop=stop), *after)

        def mmq(o, l, r, start, stop, *after):
            pe.silent(lambda e: e.matmul(o, l, r, start=start, stop=stop), *after)

        def product(o, lhs, rhs, kt, *after, by_k=None):
            pe.wait(*after)
            n, total = 0, 3 * kt
            t = None
            for k in range(kt):
                (lh, ll), (rh, rl) = lhs(k), rhs(k)
                if by_k is not None:
                    pe.wait(*by_k[k])
                for a, b in ((lh, rh), (lh, rl), (ll, rh)):
                    f = mm if n == total - 1 else mmq
                    t = f(o, a, b, n == 0, n == total - 1)
                    n += 1
            return t

        def act_set(n):
            act.ops.append(lambda e: e.add_instruction(mybir.InstLoadActFuncSet(
                name=nc.get_next_instruction_name(), act_func_set_id=n,
                engine=mybir.EngineType.Activation, ins=[], outs=[])))

        def tt(eng, o, a, b, op, *after):
            return eng(lambda e: e.tensor_tensor(o, a, b, op), *after)

        def ts(eng, o, a, s1, s2, op0, op1, *after):
            if s2 is None:
                return eng(lambda e: e.tensor_scalar(o, a, s1, None, op0), *after)
            return eng(lambda e: e.tensor_scalar(o, a, s1, s2, op0, op1), *after)

        def stt(o, a, s, b, op0, op1, *after):
            return dve(lambda e: e.scalar_tensor_tensor(o, a, s, b, op0, op1), *after)

        def af(o, i, f, *after, scale=1.0, bias=None, accum=None):
            kw = {}
            if bias is not None:
                kw["bias"] = bias
            if accum is not None:
                kw["accum_out"] = accum
            return act(lambda e: e.activation(o, i, f, scale=scale, **kw), *after)

        def copy(eng, o, i, *after):
            return eng(lambda e: e.tensor_copy(o, i), *after)

        def fill(o, v, *after):
            return pool(lambda e: e.memset(o, v), *after)

        def rmax(o, i, *after):
            return dve(lambda e: e.reduce_max(o, i, AXX), *after)

        def rsum(o, i, *after):
            return dve(lambda e: e.reduce_sum(o, i, AXX), *after)

        def recip(o, i, *after):
            return dve(lambda e: e.reciprocal(o, i), *after)

        def flip(o, i, *after):
            return pe(lambda e: e.transpose(o, i, C("ident")), *after)

        def barrier():
            flush()
            now = [e.last() for e in engines]
            for e in engines:
                e.wait(*[t for t in now if t[2] != e.name or e is not pe])
            assert not any(held)
            for i in range(8):
                bank_free[i] = list(now)
            return now

        act_set(SET_EXP_LN)
        t_ones = pool(lambda e: e.memset(ones[:, :], 1.0))
        t_mi = pool(lambda e: e.memset(mi[:, 0:1], EPS))
        eps = mi[:, 0:1]

        def split_act(hi, lo, src, *after):
            a = af(hi, src, ACT.Copy, *after)
            b = tt(dve, lo, src, hi.bitcast(F32), ALU.subtract, a, *after)
            return a, b

        def rsqrt(o, src, scale, *after):
            a = af(o, src, ACT.Ln, t_mi, *after, scale=scale, bias=eps[0:o.shape[0], :])
            return a, af(o, o, ACT.Exp, a, scale=-0.5)

        def rms_rows(x, n, *after):
            b, ps, free = bank()
            prev = [None, None]
            t = None
            act.wait(dve.last(), pe.last())
            for k in range(KT):
                s = sq[:, k % 2, 0:n]
                a = af(s, x[:, k, :], ACT.Square, prev[k % 2], *after)
                prev[k % 2] = t = mm(ps[:, 0:n], ones[:, :], s, k == 0, k == KT - 1, a, t_ones, *free)
            a, t = rsqrt(rs[:, 0:n], ps[:, 0:n], 1.0 / 1024, t)
            release(b, a)
            return t

        def norm_mod(x, n, av, bv, dst, *after):
            t_rs = rms_rows(x, n, *after)
            hist = [None, None]
            toks = []
            for k in range(KT):
                s = sq[:, k % 2, 0:n]
                hi, lo = dst[:, 0, k, :], dst[:, 1, k, :]
                y = tt(pool, s, x[:, k, :], rs[:, 0:n], ALU.mult, t_rs, *(hist[k % 2] or []))
                a = af(hi, s, ACT.Identity, y, scale=av(k), bias=bv(k))
                b = ts(dve, s, s, av(k), bv(k), ALU.mult, ALU.add, a)
                c = tt(dve, lo, s, hi.bitcast(F32), ALU.subtract, b)
                hist[k % 2] = [c]
                toks.append([a, c])
            return toks

        def pair(tile, k, sl=slice(None)):
            return tile[:, 0, k, sl], tile[:, 1, k, sl]

        c32 = ar[:, 16128:16384].rearrange("p (k j) -> p k j", j=32)

        def ada_start(cv, t_par, after):
            a = fill(c32.rearrange("p k j -> p (k j)"), 0.0, *after)
            u = mvec[:, 40:56].rearrange("p (k j) -> p k j", j=2)
            a1 = af(u, cv, ACT.Abs, t_par, *after)
            a1 = af(u, u, ACT.Exp, a1, scale=-1.0)
            a1 = af(u, u, ACT.Ln, a1, bias=1.0)
            a1 = stt(u, cv, 0.0, u, ALU.min, ALU.subtract, a1)
            a1 = af(u, u, ACT.Exp, a1)
            return tt(dve, c32[:, :, 0:2], cv, u, ALU.mult, a, a1)

        def ada_block(srcs, blk, dst, bias, t_c):
            w, t_w, done = load(srcs[blk], 4096)
            yield
            wv = w.rearrange("p (k c) -> p k c", k=KT)
            b, ps, free = bank()
            for k in range(KT):
                g = (k % 4) * 32
                f = mm if k == KT - 1 else mmq
                t = f(ps[g:g + 32, :], c32[:, k, :], wv[:, k, :], k < 4, k >= 4, t_c, t_w, *free)
            done(t)
            yield
            r = ada_row
            a = af(r, ps, ACT.Copy, t, ada_last[0])
            release(b, a)
            yield
            b, ps, free = bank()
            for m in range(4):
                t = flip(ps[:, m * 128:m * 128 + 128], r[:, m * 128:m * 128 + 128], a, t_cst, *free)
            ada_last[0] = t
            yield
            o = dst[:, 4 * blk:4 * blk + 4, :]
            a = rsum(o, ps.rearrange("p (m g j) -> p m j g", m=4, g=4)[:, :, 0:2, :], t)
            release(b, a)
            bb = bias[:, 4 * blk:4 * blk + 4].rearrange("p (m o) -> p m o", o=1).to_broadcast([P, 4, 2])
            ada_done[0] = tt(dve, o, o, bb, ALU.add, a)
            yield

        ada_row = ar[:, 12288:12800]
        ada_last = [None]
        ada_done = [None]

        def gain(o, part, j, g, t_mod):
            return stt(o, mod[:, part * 8:part * 8 + 8, j], 1.0, g, ALU.add, ALU.mult, t_mod)

        po = offsets(PAR1)
        t_par = d_small[2].start(pool, par1[:, :], I["par1"])
        t_par2 = d_small[6].start(pool, par2[:, :, :], I["par2"])
        mod = mods[:, 0, :, :]

        def Q(name):
            a, w = po[name]
            return par1[:, a:a + w]

        YA = REST - 2048
        cx = ar[:, YA:YA + 2048].rearrange("p (k n) -> p k n", k=KT)
        t_cx = d_small[3].start(pool, cx, I["ctxT"])
        cs1 = ar[:, 14592:15616].rearrange("p (k n) -> p k n", k=2)
        t_cs1 = d_small[4].start(pool, cs1, I["rope1"])
        wab = ar[:, 15616:16000].rearrange("p (k n) -> p k n", k=KT)
        t_wab = d_small[5].start(pool, wab, I["w_ab"])
        po2 = offsets(PAR2)

        def Q2(name, layer):
            a, w = po2[name]
            return par2[:, layer, a:a + w]

        c8 = lambda v: v.rearrange("p (k j) -> p k j", j=2)
        t_c = ada_start(c8(Q("c")), t_par, [])
        for blk in range(4):
            later(ada_block(I["w_ada"], blk, mod, Q("bada"), t_c))
        flush()
        t_mod = ada_done[0]
        A1, A1c, A2 = mvec[:, 0:8], mvec[:, 8:16], mvec[:, 16:24]
        t_a1 = gain(A1, 1, 0, Q("gn1"), t_mod)
        t_a1c = gain(A1c, 1, 1, Q("gn1"), t_mod)
        col = lambda v, k: v[:, k:k + 1]
        t_hc = norm_mod(cx, TC, lambda k: col(A1c, k), lambda k: mod[:, k, 1:2], hc1, t_cx, t_a1c, t_mod)
        t_h = norm_mod(xT, T, lambda k: col(A1, k), lambda k: mod[:, k, 0:1], hh, t_x, t_a1, t_mod)

        def part(at, k, n):
            return ar[:, at:at + k * n].rearrange("p (k n) -> p k n", k=k)

        kT, kTc = part(4096, 4, T), part(6144, 4, TC)
        qT = part(7168, 4, T)
        vT, vTc = part(9216, 4, T), part(11264, 4, TC)
        abr = ar[:, 12288:13056]
        ka, kac = ar[:, 13056:13568], ar[:, 13568:13824]
        va = part(13824, 6, 128)
        ya = qa = part(YA, 4, T)

        def conv(ps, n, j, dst, t, b):
            w = Q("convw")
            a = af(dst, ps[:, 0:n], ACT.Identity, t, t_par, scale=w[:, 12 + j:13 + j])
            a = stt(dst[:, 1:n], ps[:, 0:n - 1], w[:, j:j + 1], dst[:, 1:n], ALU.mult, ALU.add, a)
            a = stt(dst[:, 0:n - 1], ps[:, 1:n], w[:, 24 + j:25 + j], dst[:, 0:n - 1], ALU.mult, ALU.add, a)
            release(b, a)
            return a

        def head_rope(ps, n, g, dst, t, b, roped, tables, t_tab, perm, end=None):
            a = af(dst, ps[:, 0:n], ACT.Copy, t)
            if g is not None:
                s = sq[:, 0, 0:n]
                a2 = af(s, ps[:, 0:n], ACT.Square, t, pe.last(), dve.last())
                release(b, a2)
                b1, p1, free = bank()
                m = mm(p1[:, 0:n], C("bd"), s, True, True, a2, t_cst, *free)
                yield
                r = sq[:, 1, 0:n]
                e0, e1 = rsqrt(r, p1[:, 0:n], 1.0 / 64, m, dve.last())
                release(b1, e0)
                a = stt(dst, dst, g, r, ALU.mult, ALU.mult, a, e1)
            else:
                release(b, a)
            if roped:
                yield
                b2, p2, free = bank()
                m = mm(p2[:, 0:n], C(perm), dst, True, True, a, t_cst, *free)
                yield
                r = sq[:, 1, 0:n]
                a1 = tt(dve, r, p2[:, 0:n], tables[:, 1, 0:n], ALU.mult, m, t_tab, act.last())
                release(b2, a1)
                a2 = tt(dve, dst, dst, tables[:, 0, 0:n], ALU.mult, a, m, t_tab)
                a = tt(dve, dst, dst, r, ALU.add, a1, a2)
            if end is not None:
                end[0] = a

        coming(I["w_kv"], cols=256)
        coming(*(I["w_1"][i] for i in range(4)))
        s, hi, lo, t_hi, t_lo = piece()
        lw = lambda k, hi=hi, lo=lo: (hi[:, k, :], lo[:, k, :])
        bk, pk, free = bank()
        tk = product(pk[:, 0:T], lw, lambda k: pair(hh, k), KT, t_hi, t_lo, *free, by_k=t_h)
        bkc, pkc, free = bank()
        tkc = product(pkc[:, 0:TC], lw, lambda k: pair(hc1, k), KT, *free, by_k=t_hc)
        ws_free[s] = tkc
        t_ka, t_kac = [None], [None]
        later(head_rope(pk, T, Q("kg"), ka, tk, bk, True, cs1, t_cs1, "perm1", t_ka))
        later(head_rope(pkc, TC, Q("kg"), kac, tkc, bkc, False, None, None, None, t_kac))
        s, hi, lo, t_hi, t_lo = piece()
        rw = lambda k, hi=hi, lo=lo: (hi[:, k, :], lo[:, k, :])
        b, ps, free = bank()
        for i in range(4):
            t = product(ps[:, i * 128:i * 128 + 128], lambda k: pair(hh, k, slice(i * 128, i * 128 + 128)), rw, KT,
                        t_hi, t_lo, *free)
        bc, psc, free = bank()
        for i in range(2):
            t2 = product(psc[:, i * 128:i * 128 + 128], lambda k: pair(hc1, k, slice(i * 128, i * 128 + 128)), rw,
                         KT, *free)
        ws_free[s] = t2
        t_va = af(va[:, 0:4, :].rearrange("p t n -> p (t n)"), ps[:, :], ACT.Copy, t, *t_hc[-1])
        t_vac = af(va[:, 4:6, :].rearrange("p t n -> p (t n)"), psc[:, 0:TC], ACT.Copy, t2)
        release(b, t_va)
        release(bc, t_vac)
        flush()
        hsum = sq
        b, ps, free = bank()
        hist = [None, None]
        lat = None
        for src, n, at in ((hh, T, 0), (hc1, TC, T)):
            if at:
                b2, ps2, free = bank()
            else:
                b2, ps2 = b, ps
            for k in range(KT):
                f = hsum[:, k % 2, 0:n]
                a = tt(dve, f, src[:, 0, k, :].bitcast(F32), src[:, 1, k, :].bitcast(F32), ALU.add,
                       hist[k % 2], *t_h[-1], *t_hc[-1], act.last(), pe.last() if k == 0 else None)
                hist[k % 2] = t = mm(ps2[0:48, 0:n], wab[:, k, :], f, k == 0, k == KT - 1, a, t_wab, *free)
            t1 = abr[0:48, 0:n] if not at else None
            x1 = abr[0:48, 0:768][:, at:at + n]
            x2 = sq[0:48, 0, 0:n]
            a = af(x1, ps2[0:48, 0:n], ACT.Identity, t, t_par, bias=Q("dtb")[0:48, :])
            release(b2, a)
            a = af(x2, x1, ACT.Abs, a, hist[0], hist[1])
            a = af(x2, x2, ACT.Exp, a, scale=-1.0)
            a = af(x2, x2, ACT.Ln, a, bias=1.0)
            if not at:
                ea = mi[0:32, 1:2]
                t_ea = af(ea, Q("alog")[0:32, :], ACT.Exp, t_par)
                t_ea = ts(dve, ea, ea, -1.0, None, ALU.mult, None, t_ea)
            c1 = stt(x1[0:32, :], x1[0:32, :], 0.0, x2[0:32, :], ALU.max, ALU.add, a)
            c1 = ts(dve, x1[0:32, :], x1[0:32, :], ea, None, ALU.mult, None, c1, t_ea)
            c2 = stt(x1[32:48, :], x1[32:48, :], 0.0, x2[32:48, :], ALU.min, ALU.subtract, a)
            c2 = af(x1[32:48, :], x1[32:48, :], ACT.Exp, c2)
            hist = [c1, c1]
        t_ab = [c1, c2]

        def tiles_of(n, streams, evac, pre=(), kt=KT, by_k=None):
            for m in range(n):
                s, hi, lo, t_hi, t_lo = piece()
                for j, (rhs, w) in enumerate(streams):
                    b, ps, free = bank()
                    t = product(ps[:, 0:w], lambda k: (hi[:, k, :], lo[:, k, :]), rhs, kt, t_hi, t_lo, *pre, *free,
                                by_k=by_k[j] if by_k else None)
                    if j == len(streams) - 1:
                        ws_free[s] = t
                    later(evac(m, j, ps, t, b))

        rh = lambda k: pair(hh, k)
        rc1 = lambda k: pair(hc1, k)

        def ev_q(m, j, ps, t, b):
            return head_rope(ps, T, Q("qg"), qa[:, m, :], t, b, True, cs1, t_cs1, "perm1")
        tiles_of(4, [(rh, T)], ev_q)

        def conv_ev(dst, dstc, base):
            def ev(m, j, ps, t, b):
                if j == 0:
                    conv(ps, T, base + m, dst[:, m, :], t, b)
                else:
                    conv(ps, TC, base + m, dstc[:, m, :], t, b)
            return ev
        tiles_of(4, [(rh, T), (rc1, TC)], conv_ev(kT, kTc, 4))
        tiles_of(4, [(rh, T), (rc1, TC)], conv_ev(vT, vTc, 8))
        tiles_of(4, [(rh, T)], conv_ev(qT, None, 0))

        barrier()
        pbuf = [ar[:, i * 640:(i + 1) * 640] for i in range(2)]
        ptb = [ar[:, 1280 + i * 640:1280 + (i + 1) * 640].rearrange("p (j q) -> p j q", j=5) for i in range(2)]
        small = mvec[:, 24:40]
        p_free = [None, None]
        pt_free = [None, None]
        items = [(qb, h) for qb in range(4) for h in range(8)]
        st = {}

        def scores(i):
            qb, h = items[i]
            t4, p = h % 4, h // 4
            q = qa[p * 64:p * 64 + 64, t4, qb * 128:qb * 128 + 128]
            b, ps, free = bank2()
            kr = slice(p * 64, p * 64 + 64)
            mm(ps[:, 0:256], q, kac[kr, :], True, True, *free)
            at = 256
            tiles = []
            for kb in range(max(0, qb - 1), min(4, qb + 2)):
                o_ = ps[:, at:at + 128]
                tiles.append(kb)
                masked = kb != qb
                t = mm(o_, q, ka[kr, kb * 128:kb * 128 + 128], True, not masked)
                if masked:
                    t = mm(o_, C("ident"), C("mprev" if kb < qb else "mnext"), False, True)
                at += 128
            st[i] = (b, ps, at, tiles, t)

        def soft(i):
            qb, h = items[i]
            b, ps, n, tiles, t = st[i]
            sm = small[:, (i % 2) * 8:(i % 2) * 8 + 8]
            mx, nm, su, es, rc = (sm[:, k:k + 1] for k in range(5))
            sink = Q("sink")[:, h:h + 1]
            a = rmax(mx, ps[:, 0:n], t, p_free[i % 2])
            a = ts(dve, nm, mx, 0.125, sink, ALU.mult, ALU.max, a)
            a = ts(dve, nm, nm, -1.0, None, ALU.mult, None, a)
            pb = pbuf[i % 2][:, 0:n]
            a1 = af(pb, ps[:, 0:n], ACT.Exp, a, p_free[i % 2], scale=0.125, bias=nm, accum=su)
            release2(b, a1)
            a2 = af(es, sink, ACT.Exp, a, bias=nm)
            a = tt(dve, su, su, es, ALU.add, a1, a2)
            a = recip(rc, su, a)
            a = ts(dve, pb, pb, rc, None, ALU.mult, None, a)
            st[i] = (pb, n, tiles, a)

        ops = {}

        def outp(i):
            qb, h = items[i]
            t4, p = h % 4, h // 4
            pb, n, tiles, a = st.pop(i)
            nt = n // 128
            b, ps, free = bank2()
            for j in range(nt):
                t = flip(ps[:, j * 128:j * 128 + 128], pb[:, j * 128:j * 128 + 128], a, *free)
            p_free[i % 2] = t
            pt = ptb[i % 2]
            c = af(pt[:, 0:nt, :].rearrange("p j q -> p (j q)"), ps[:, 0:n], ACT.Copy, t, pt_free[i % 2])
            release2(b, c)
            if h == 0:
                ops[qb] = bank_held()
            b, ps, free = ops[qb]
            for j in range(nt):
                vt = va[:, 4 + j, p * 64:p * 64 + 64] if j < 2 else va[:, tiles[j - 2], p * 64:p * 64 + 64]
                t = mm(ps[p * 64:p * 64 + 64, t4 * 128:t4 * 128 + 128], vt, pt[:, j, :], j == 0, j == nt - 1,
                       c, t_va, t_vac, *free)
            pt_free[i % 2] = t
            if h == 7:
                c = copy(dve, ya[:, :, qb * 128:qb * 128 + 128], ps.rearrange("p (t q) -> p t q", t=4), t)
                release(b, c)

        rotating[0] = 6
        scores(0)
        for i in range(32):
            if i < 31:
                scores(i + 1)
            soft(i)
            if i:
                outp(i - 1)
        outp(31)
        rotating[0] = 8
        barrier()

        act_set(SET_SIGMOID)
        sg = [ar[:, i * 512:(i + 1) * 512] for i in range(4)]
        use = [None] * 4
        jobs = [(kT, m, T) for m in range(4)] + [(vT, m, T) for m in range(4)] + [(qT, m, T) for m in range(4)] \
            + [(kTc, m, TC) for m in range(4)] + [(vTc, m, TC) for m in range(4)]
        for i, (tl, m, n) in enumerate(jobs):
            s = sg[i % 4][:, 0:n]
            a = af(s, tl[:, m, :], ACT.Sigmoid, use[i % 4])
            use[i % 4] = tt(dve, tl[:, m, :], tl[:, m, :], s, ALU.mult, a)
        act_set(SET_EXP_LN)
        t_silu = dve.last()
        for i, (tl, m, n) in enumerate([j for j in jobs if j[0] is not vT and j[0] is not vTc]):
            s = sg[i % 2][:, 0:n]
            r = sg[2 + i % 2][:, 0:n]
            a = af(s, tl[:, m, :], ACT.Square, t_silu, use[i % 2])
            b, ps, free = bank()
            t = mm(ps[:, 0:n], C("bd"), s, True, True, a, *free)
            e0, e1 = rsqrt(r, ps[:, 0:n], 1.0, t)
            release(b, e0)
            if tl is qT:
                use[i % 2] = stt(tl[:, m, :], tl[:, m, :], 0.125, r, ALU.mult, ALU.mult, e1)
            else:
                use[i % 2] = tt(dve, tl[:, m, :], tl[:, m, :], r, ALU.mult, e1)
        barrier()

        ktok = ar[:, 0:3072].rearrange("p (n r v) -> p n r v", n=12, r=4)
        vtok = ar[:, 13056:16128].rearrange("p (n r v) -> p n r v", n=12, r=4)
        for src, srcc, dst in ((kT, kTc, ktok), (vT, vTc, vtok)):
            for n2 in range(6):
                b, ps, free = bank()
                for half in range(2):
                    n = 2 * n2 + half
                    tl, at = (src, n * 64) if n < 8 else (srcc, (n - 8) * 64)
                    for pr in range(4):
                        for p in range(2):
                            sl = slice(p * 64, p * 64 + 64)
                            t = mm(ps[sl, (half * 4 + pr) * 64:(half * 4 + pr) * 64 + 64],
                                   tl[sl, pr, at:at + 64], C("i64")[sl, :], True, True, *free)
                d = dst[:, 2 * n2:2 * n2 + 2, :, :].rearrange("p n r v -> p (n r v)")
                if n2 % 2:
                    c = copy(dve, d, ps, t)
                else:
                    c = af(d, ps, ACT.Copy, t)
                release(b, c)
        barrier()
        gate = rs[:, 0:192].rearrange("p (s b d r) -> p s b d r", s=12, b=2, d=2)
        b, ps, free = bank()
        pg = ps[:, 0:192].rearrange("p (s b d r) -> p s b d r", s=12, b=2, d=2)
        sel = C("sel").rearrange("p (q b d r) -> p q b d r", q=2, b=2, d=2)

        def chunk_of(s, d):
            if s < 4:
                return 8 + (s if d == 0 else 3 - s)
            return s - 4 if d == 0 else 11 - s

        for s in range(12):
            for d in range(2):
                n = chunk_of(s, d)
                at = n * 64
                for p in range(2):
                    sl = slice(p * 64, p * 64 + 64)
                    t = mm(pg[sl, s, :, d, :], abr[0:48, at:at + 64], sel[0:48, p, :, d, :], True, True, *free)
        t = copy(dve, rs[:, 0:192], ps[:, 0:192], t)
        release(b, t)
        t_gate = t
        b, ps, free = bank()
        gcp = ps[:, 0:96].rearrange("p (s d r) -> p s d r", s=12, d=2)
        glp = ps[:, 96:192].rearrange("p (s d r) -> p s d r", s=12, d=2)
        mm(gcp[:, :, 0, :], C("trif"), gate[:, :, 0, 0, :], True, True, t_gate, *free)
        mm(gcp[:, :, 1, :], C("trib"), gate[:, :, 0, 1, :], True, True)
        t = mm(glp, C("bd"), gate[:, :, 0, :, :], True, True)
        gt = rs[:, 192:512]
        Gc = sq[:, 0, 0:96].rearrange("p (s x) -> p s x", s=12)
        eG = sq[:, 0, 96:192].rearrange("p (s x) -> p s x", s=12)
        tail = sq[:, 0, 192:288].rearrange("p (s x) -> p s x", s=12)
        egl = sq[:, 0, 288:384].rearrange("p (s x) -> p s x", s=12)
        beG = sq[:, 0, 384:480].rearrange("p (s x) -> p s x", s=12)
        bet = rs[:, 192:288].rearrange("p (s x) -> p s x", s=12)
        flat = lambda v: v.rearrange("p s x -> p (s x)")
        a = copy(dve, flat(Gc), ps[:, 0:96], t)
        a2 = tt(dve, flat(tail), ps[:, 96:192], flat(Gc), ALU.subtract, a)
        a3 = af(flat(egl), ps[:, 96:192], ACT.Exp, t, a2)
        release(b, a3)
        a4 = af(flat(tail), flat(tail), ACT.Exp, a2)
        a5 = af(flat(eG), flat(Gc), ACT.Exp, a)
        a6 = copy(dve, bet.rearrange("p s (d r) -> p s d r", d=2), gate[:, :, 1, :, :], t_gate)
        a7 = tt(dve, flat(beG), flat(bet), flat(eG), ALU.mult, a5, a6)
        barrier()

        X3 = "p (x v) -> p x v"
        sA, sX, sXt, sV, sIT, sE = (ar[:, 9216 + i * 512:9728 + i * 512].rearrange(X3, x=8) for i in range(6))
        slot, slot_free, slot_done = reserve()
        sKt, sR, sU, sT2 = (slot[:, i * 512:(i + 1) * 512].rearrange(X3, x=8) for i in range(4))
        oacc = slot[:, 2048:4096].rearrange("p (n r v) -> p n r v", n=8, r=4)
        for e in engines:
            e.wait(*slot_free)
        sVb = sq[:, 1, :].rearrange(X3, x=8)
        sS = ar[:, 3072:3584].rearrange(X3, x=8)
        sD = ar[:, 3584:4096].rearrange(X3, x=8)
        t_S = fill(sS.rearrange("p x v -> p (x v)"), 0.0)
        i64b = C("i64").rearrange("p (o v) -> p o v", o=1).to_broadcast([P, 8, 64])
        lv = C("lvl").rearrange("p (l v) -> p l v", l=6)

        def lvb(l):
            return lv[:, l:l + 1, :].to_broadcast([P, 8, 64])

        mst = C("mstrict").rearrange("p (d v) -> p d v", d=2)
        min_ = C("mincl").rearrange("p (d v) -> p d v", d=2)

        def rowb(tb, s, x0=0, x1=8):
            return tb[:, s, x0:x1].rearrange("p (x o) -> p x o", o=1).to_broadcast([P, x1 - x0, 64])

        def tile_src(tl, tlc, n):
            return (tl, n * 64) if n < 8 else (tlc, (n - 8) * 64)

        def quad(o_, l, r, *after):
            t = None
            for x in range(8):
                for p in range(2):
                    sl = slice(p * 64, p * 64 + 64)
                    last = x == 7 and p == 1
                    f = mm if last else mmq
                    t = f(o_[sl, x * 64:x * 64 + 64], l(x, sl), r(x, sl), True, True, *after)
            return t

        comp = lambda tb: (lambda x, sl: tb[sl, x, :])
        v3 = lambda ps: ps.rearrange(X3, x=8)
        ada_jobs = [(I["w_ada"], blk, mods[:, 0, :, :], Q("bada")) for blk in range(4, 12)]
        ada_jobs += [(I[n_], blk, mods[:, 1 + l_, :, :], Q2("bada", l_)) for l_, n_ in enumerate(("w_ada2_0", "w_ada2_1"))
                     for blk in range(12)]
        t_c2 = [t_c]

        def ada_slot():
            if len(ada_jobs) == 24:
                flush()
                t_c2[0] = ada_start(c8(Q2("c", 0)), t_par2, [pe.last(), dve.last()])
            later(ada_block(*ada_jobs.pop(0), t_c2[0]) if ada_jobs else None)

        t_prev = {}
        g = lambda k: t_prev.get(k)

        for s in range(12):
            ch = [chunk_of(s, 0), chunk_of(s, 1)]
            kf = lambda x, sl: (lambda ta: ta[0][sl, x % 4, ta[1]:ta[1] + 64])(tile_src(kT, kTc, ch[x // 4]))
            qf = lambda x, sl: qT[sl, x % 4, ch[x // 4] * 64:ch[x // 4] * 64 + 64]
            latent = s >= 4
            a = tt(dve, sD, i64b, rowb(Gc, s), ALU.mult, g("D"))
            bg, pg_, free = bank()
            tg = mm(pg_, C("bd"), sD.rearrange("p x v -> p (x v)"), True, True, a, *free)
            a1 = tt(dve, sD, rowb(Gc, s), v3(pg_), ALU.subtract, tg)
            release(bg, a1)
            for d in range(2):
                a2 = tt(dve, sE[:, 4 * d:4 * d + 4, :], sD[:, 4 * d:4 * d + 4, :],
                        mst[:, d:d + 1, :].to_broadcast([P, 4, 64]), ALU.add, a1, g("E"))
            a3 = af(sE.rearrange("p x v -> p (x v)"), sE.rearrange("p x v -> p (x v)"), ACT.Exp, a2)
            bkk, pkk, free = bank()
            tkk = quad(pkk, kf, kf, *free)
            a4 = tt(dve, sA, sE, v3(pkk), ALU.mult, a3, tkk, g("A"))
            release(bkk, a4)
            tA = tt(dve, sA, sA, rowb(bet, s), ALU.mult, a4)
            if latent:
                bqk, pqk, free = bank()
                tqk = quad(pqk, kf, qf, *free)
                for d in range(2):
                    a5 = tt(dve, sIT[:, 4 * d:4 * d + 4, :], min_[:, d:d + 1, :].to_broadcast([P, 4, 64]),
                            sD[:, 4 * d:4 * d + 4, :], ALU.subtract, a1, g("IT"))
                a6 = af(sIT.rearrange("p x v -> p (x v)"), sIT.rearrange("p x v -> p (x v)"), ACT.Exp, a5)
                tIT = tt(dve, sIT, sIT, v3(pqk), ALU.mult, a6, tqk)
                release(bqk, tIT)
            for d in range(2):
                xs = slice(4 * d, 4 * d + 4)
                tKt = tt(pool, sKt[:, xs, :], ktok[:, ch[d], :, :], rowb(tail, s, 4 * d, 4 * d + 4), ALU.mult,
                         g("Kt"))
                tVb = tt(pool, sVb[:, xs, :], vtok[:, ch[d], :, :], rowb(bet, s, 4 * d, 4 * d + 4), ALU.mult,
                         g("Vb"))
            ada_slot()
            bv, pv, free = bank()
            tv = quad(pv, comp(sA), lambda x, sl: C("i64")[sl, :], tA, *free)
            a = tt(dve, sV, v3(pv), lvb(0), ALU.mult, tv)
            release(bv, a)
            tXt = tt(dve, sXt, i64b, sV, ALU.subtract, a, g("Xt"))
            a = tt(pool, sX, sA, lvb(0), ALU.mult, tA)
            tX = tt(pool, sX, i64b, sX, ALU.subtract, a)
            for l in range(1, 6):
                bv, pv, free = bank()
                tv = quad(pv, comp(sA), comp(sXt), tXt, *free)
                tV = tt(dve, sV, v3(pv), lvb(l), ALU.mult, tv)
                release(bv, tV)
                bz, pz, free = bank()
                tz = quad(pz, comp(sX), comp(sV), tV, tX, *free)
                tXt = tt(dve, sXt, sXt, v3(pz), ALU.subtract, tz)
                release(bz, tXt)
                if l == 3:
                    ada_slot()
                if l < 5:
                    bz, pz, free = bank()
                    tz = quad(pz, comp(sV), comp(sX), *free)
                    tX = tt(dve, sX, sX, v3(pz), ALU.subtract, tz)
                    release(bz, tX)
            ada_slot()
            bs, psS, free = bank()
            t = quad(psS, kf, comp(sS), t_S, *free)
            a = tt(dve, sR, v3(psS), rowb(beG, s), ALU.mult, t)
            release(bs, a)
            tR = tt(dve, sR, sVb, sR, ALU.subtract, a, tVb)
            bu, pu, free = bank()
            t = quad(pu, comp(sXt), comp(sR), tR, tXt, *free)
            tU = af(sU.rearrange("p x v -> p (x v)"), pu, ACT.Copy, t)
            release(bu, tU)
            bd_, pd, free = bank()
            tdS = quad(pd, comp(sKt), comp(sU), tU, tKt, *free)
            if latent:
                bq, pq, free = bank()
                t = quad(pq, qf, comp(sS), *free)
                a = tt(dve, sT2, v3(pq), rowb(eG, s), ALU.mult, t, g("T2"))
                release(bq, a)
                bi, pi, free = bank()
                t = quad(pi, comp(sIT), comp(sU), tIT, *free)
                tT = tt(dve, sT2, sT2, v3(pi), ALU.add, a, t)
                release(bi, tT)
                for d in range(2):
                    xs = slice(4 * d, 4 * d + 4)
                    dst = oacc[:, ch[d], :, :]
                    if s < 8:
                        t = copy(pool, dst, sT2[:, xs, :], tT)
                    else:
                        t = tt(pool, dst, dst, sT2[:, xs, :], ALU.add, tT)
                t_prev["T2"] = t
                t_prev["IT"] = pe.last()
            if s < 11:
                a = tt(dve, sS, sS, rowb(egl, s), ALU.mult, pe.last())
                t_S = tt(dve, sS, sS, v3(pd), ALU.add, a, tdS)
                release(bd_, t_S)
            else:
                release(bd_, tdS)
            t_prev.update(D=dve.last(), E=tA, A=pe.last(), Kt=tdS, Vb=tR, Xt=pe.last())
        while pending or ada_jobs:
            ada_slot()
        gain(A2, 4, 0, Q("gn2"), ada_done[0])
        barrier()
        t_cst2 = d_small[7].start(pool, cst[:, CW - CW2:CW], I["consts2"])

        of = oacc.rearrange("p n r v -> p (n r) v")
        o2f = ar[:, 0:2048].rearrange("p (n v) -> p n v", v=64)
        a = tt(dve, o2f, of, of, ALU.mult)
        ssum = mvec[:, 24:56]
        a = rsum(ssum, o2f, a)
        _, a = rsqrt(ssum, ssum, 1.0 / 64, a)
        a = tt(dve, of, of, ssum.rearrange("p (x o) -> p x o", o=1).to_broadcast([P, 32, 64]), ALU.mult, a)
        yd = part(8192, 4, T)
        for pr in range(4):
            b, ps, free = bank()
            for n in range(8):
                for p in range(2):
                    sl = slice(p * 64, p * 64 + 64)
                    t = mm(ps[sl, n * 64:n * 64 + 64], oacc[sl, n, pr, :], C("i64")[sl, :], True, True, a, *free)
            c = ts(dve, yd[:, pr, :], ps, Q("dng"), None, ALU.mult, None, t)
            release(b, c)
        barrier()
        slot_done(pe.last())
        act_set(SET_SIGMOID)

        def ev_z(m, j, ps, t, b):
            s0 = sq[:, m % 2, :]
            a = af(s0, ps, ACT.Sigmoid, t, dve.last())
            a = tt(dve, s0, s0, ps, ALU.mult, a)
            release(b, a)
            a = tt(dve, yd[:, m, :], yd[:, m, :], s0, ALU.mult, a)
            split_act(gg[:, 0, 4 + m, :], gg[:, 1, 4 + m, :], yd[:, m, :], a)
        coming(I["w_1"][4])
        coming(*(I["w_mg"][i] for i in range(8)), cols=384)
        coming(*(I["w_out"][i] for i in range(2)))
        tiles_of(4, [(rh, T)], ev_z)
        for m in range(4):
            split_act(gg[:, 0, m, :], gg[:, 1, m, :], ya[:, m, :])
        t_gg = barrier()

        for half in range(2):
            for m in range(4):
                mt = half * 4 + m
                res = []
                for i in range(3):
                    s, hi, lo, t_hi, t_lo = piece()
                    if i < 2:
                        b, ps, free = bank()
                        t = product(ps, lambda k: (hi[:, k, :], lo[:, k, :]), rh, KT, t_hi, t_lo, *free)
                        res.append((b, ps, t))
                    else:
                        for h0 in (0, 4):
                            b, ps, free = bank()
                            t = product(ps, lambda k: (hi[:, h0 + k, :], lo[:, h0 + k, :]),
                                        lambda k: pair(gg, h0 + k), 4, t_hi, t_lo, *free)
                            res.append((b, ps, t))
                    ws_free[s] = t
                (b0, p0, t0), (b1, p1, t1_), (b2, p2, t2), (b3, p3, t3) = res
                u0, u1 = sq[:, 0, :], sq[:, 1, :]
                a = af(u0, p0, ACT.Sigmoid, t0, act.last(), dve.last())
                release(b0, a)
                c = af(u1, p1, ACT.Sigmoid, t1_)
                release(b1, c)
                a = tt(dve, u0, u0, p2, ALU.mult, a, t2)
                release(b2, a)
                c = tt(dve, u1, u1, p3, ALU.mult, c, t3)
                release(b3, c)
                a = tt(dve, u0, u0, u1, ALU.add, a, c)
                split_act(yy[:, 0, mt, :], yy[:, 1, mt, :], u0, a)
        act_set(SET_EXP_LN)
        t_yy = [act.last(), dve.last()]

        def residual(xt, n, part, j):
            def ev(base):
                def f(m, jj, ps, t, b):
                    mt = base + m
                    c = stt(xt[:, mt, 0:n], ps[:, 0:n], mod[:, part * 8 + mt, j:j + 1], xt[:, mt, 0:n],
                            ALU.mult, ALU.add, t, dve.last())
                    release(b, c)
                return f
            return ev

        ry = lambda k: pair(yy, k)
        for half in range(2):
            tiles_of(4, [(ry, T)], residual(xT, T, 2, 0)(half * 4), pre=t_yy)

        def mlp_blocks(w1, w2):
            for q in range(4):
                coming(w1[2 * q], w1[2 * q + 1], w2[2 * q], w2[2 * q + 1])

        def mlp(streams, t_in):
            for q in range(4):
                by_k = [[] for _ in streams]

                def ev1(m, j, ps, t, b):
                    hs, hid, xt, n, mj = streams[j]
                    r = sq[:, (m + j) % 2, 0:n]
                    a = af(r, ps[:, 0:n], ACT.Relu, t, dve.last(), pool.last())
                    a2 = tt(dve, r, r, r, ALU.mult, a)
                    release(b, a)
                    by_k[j].append(split_act(hid[:, 0, m, :], hid[:, 1, m, :], r, a2))
                tiles_of(8, [((lambda k, h=st_[0]: pair(h, k)), st_[3]) for st_ in streams], ev1, by_k=t_in)
                evs = [residual(st_[2], st_[3], 5, st_[4])(0) for st_ in streams]
                tiles_of(8, [((lambda k, h=st_[1]: pair(h, k)), st_[3]) for st_ in streams],
                         lambda m, j, ps, t, b: evs[j](m, j, ps, t, b), by_k=by_k)
            flush()

        mlp_blocks(I["w_mlp1"], I["w_mlp2"])
        t_n = norm_mod(xT, T, lambda k: col(A2, k), lambda k: mod[:, 24 + k, 0:1], hh, dve.last())
        act.wait(pe.last())
        mlp([(hh, gg, xT, T, 0)], [t_n])
        barrier()

        t_cx = d_small[3].start(pool, ctx2[:, :, :], I["ctxT2"])
        for layer in range(2):
            last = layer == 1
            barrier()
            mod = mods[:, 1 + layer, :, :]
            A1, A1c, A2, A2c = (mvec[:, 8 * i:8 * i + 8] for i in range(4))
            gain(A1, 1, 0, Q2("gmix", layer), None)
            gain(A1c, 1, 1, Q2("gmix", layer), None)
            gain(A2, 4, 0, Q2("gmlp", layer), None)
            gain(A2c, 4, 1, Q2("gmlp", layer), None)
            lam_init = 0.8 - 0.6 * float(np.exp(-0.3 * layer))
            lv_ = Q2("lam", layer).rearrange("p (i q) -> p i q", i=2)
            l2 = mi[:, 2:4]
            a = tt(dve, l2, lv_[:, :, 0], lv_[:, :, 1], ALU.mult)
            b, ps, free = bank()
            t = mm(ps[:, 0:2], ones[:, :], l2, True, True, a, *free)
            a = af(l2, ps[:, 0:2], ACT.Exp, t)
            release(b, a)
            nlam = mi[:, 4:5]
            a = tt(dve, nlam, mi[:, 3:4], mi[:, 2:3], ALU.subtract, a)
            t_lam = ts(dve, nlam, nlam, -lam_init, None, ALU.add, None, a)
            gs = mi[:, 5:6]
            t_gs = ts(dve, gs, Q2("gsub", layer), 1.0 - lam_init, None, ALU.mult, None)
            barrier()
            norm_mod(ctx2, TC, lambda k: col(A1c, k), lambda k: mod[:, k, 1:2], hc2, t_cx)
            norm_mod(xT, T, lambda k: col(A1, k), lambda k: mod[:, k, 0:1], hh)

            kall = ar2[:, 0:3072].rearrange("p (t n) -> p t n", t=4)
            qc = ar2[:, 3072:4096].rearrange("p (t n) -> p t n", t=4)
            q2 = ar2[:, 4096:6144].rearrange("p (t n) -> p t n", t=4)
            vall = ar2[:, 6144:9216].rearrange("p (t n) -> p t n", t=6)
            rope = ar2[:, 9216:10240].rearrange("p (i n) -> p i n", i=2)
            wpl = ar2[:, 10240:10752].rearrange("p (i n) -> p i n", i=4)
            t_rope = d_small[4].start(pool, rope, I["rope2"], pool.last())
            t_wp = d_small[5].start(pool, wpl, I["w_pool"][layer])
            rc = lambda k: pair(hc2, k)
            pre = barrier()

            def ev_k(m, j, ps, t, b):
                if j == 0:
                    return head_rope(ps, T, None, kall[:, m, 256:768], t, b, True, rope, t_rope, "perm2")
                return head_rope(ps, TC, None, kall[:, m, 0:256], t, b, False, None, None, None)

            def ev_q2(m, j, ps, t, b):
                if j == 0:
                    return head_rope(ps, T, None, q2[:, m, :], t, b, True, rope, t_rope, "perm2")
                return head_rope(ps, TC, None, qc[:, m, :], t, b, False, None, None, None)
            W = ("w_in2_0", "w_in2_1")[layer]
            coming(I[W][2], I[W][1])
            coming(I[W][3], pk=2, pc=512)
            coming(I[W][0])
            for e in (pe, dve):
                e.wait(t_cst2)
            tiles_of(4, [(rh, T), (rc, TC)], ev_k)
            tiles_of(4, [(rh, T)] + ([] if last else [(rc, TC)]), ev_q2)
            flush()
            outs = [bank() for _ in range(6)]
            for kh in range(4):
                s, hi, lo, t_hi, t_lo = piece()
                for i in range(6):
                    b, ps, free = outs[i]
                    src, at = (hc2, i * 128) if i < 2 else (hh, (i - 2) * 128)
                    pe.wait(t_hi, t_lo, *free)
                    for kk in range(2):
                        k = 2 * kh + kk
                        lh, ll = pair(src, k, slice(at, at + 128))
                        for n_, (x_, y_) in enumerate(((lh, hi), (lh, lo), (ll, hi))):
                            f = mm if kk == 1 and n_ == 2 else mmq
                            t = f(ps, x_, y_[:, kk, :], k == 0 and n_ == 0, k == 7 and n_ == 2)
                    if kh == 3:
                        c = af(vall[:, i, :], ps, ACT.Copy, t)
                        release(b, c)
                ws_free[s] = t

            def pool_branch(m, j, ps, t, b):
                n = (T, TC)[j]
                win = (2, 4, 8, 16)[m]
                up = ar2[:, 10752:10752 + n + 32]
                two = (ar2[:, 11296:11296 + n + 32], slot[:, 3072:3072 + n + 32])
                dve.wait(pe.last())
                a = fill(up, 0.0, dve.last(), pe.last())
                for v in two:
                    z = fill(v, 0.0)
                u = af(up[:, 16:16 + n], ps[:, 0:n], ACT.Copy, t, a)
                release(b, u)
                cur, base, w_ = up, u, 1
                while w_ < win:
                    L = n + 32 - w_
                    nxt = two[0] if cur is not two[0] else two[1]
                    base = tt(dve, nxt[:, 0:L], cur[:, 0:L], cur[:, w_:w_ + L], ALU.add, base, z)
                    cur = nxt
                    w_ *= 2
                y = cur[:, 16 - win // 2:16 - win // 2 + n]
                a = ts(dve, y, y, 1.0 / win, None, ALU.mult, None, base)
                ed = C("edge").rearrange("p (g e) -> p g e", g=4)
                a = tt(dve, y[:, 0:8], y[:, 0:8], ed[:, m, 0:8], ALU.mult, a)
                a = tt(dve, y[:, n - 8:n], y[:, n - 8:n], ed[:, m, 8:16], ALU.mult, a)
                a = tt(dve, y, y, up[:, 16:16 + n], ALU.subtract, a)
                yield
                b2, p2, free = bank()
                t = mm(p2[:, 0:n], wpl[:, m, :], y, True, True, a, t_wp, *free)
                dst = mixp[:, m, 0:n] if j == 0 else mixpc[:, m, 0:n]
                c = ts(dve, dst, p2[:, 0:n], Q2("spool", layer)[:, m:m + 1], None, ALU.mult, None, t)
                release(b2, c)

            slot, slot_free, slot_done = reserve()
            mixp = slot[:, 0:2048].rearrange("p (k n) -> p k n", k=4)
            mixpc = slot[:, 2048:3072].rearrange("p (k n) -> p k n", k=4)
            for e in engines:
                e.wait(*slot_free)
            tiles_of(4, [(rh, T)] + ([] if last else [(rc, TC)]), pool_branch)
            barrier()
            for m in range(4):
                split_act(hh[:, 0, m, :], hh[:, 1, m, :], mixp[:, m, :])
                if not last:
                    split_act(hc2[:, 0, m, :], hc2[:, 1, m, :], mixpc[:, m, :])
            slot_done(*barrier())
            wo = I[("w_out2_0", "w_out2_1")[layer]]
            coming(wo[0], wo[1])
            mlp_blocks(I[("w_m1_0", "w_m1_1")[layer]], I[("w_m2_0", "w_m2_1")[layer]])

            jobs2 = [(0, qb, t4) for qb in range(4) for t4 in range(4)]
            if not last:
                jobs2 += [(1, qb, t4) for qb in range(2) for t4 in range(4)]
            e_buf = [ar2[:, 9216 + i * 768:9216 + (i + 1) * 768] for i in range(2)]
            p_t = ar2[:, 10752:10752 + 768].rearrange("p (j q) -> p j q", j=6)
            held_out = {}
            rotating[0] = 6
            st2 = {}

            def scores2(i):
                kind, qb, t4 = jobs2[i]
                n = TC if kind else 768
                qsrc = qc if kind else q2
                got = []
                for p in range(2):
                    sl = slice(p * 64, p * 64 + 64)
                    b, ps, free = bank2()
                    q = qsrc[sl, t4, qb * 128:qb * 128 + 128]
                    for a0 in range(0, n, 512):
                        a1 = min(n, a0 + 512)
                        t = mm(ps[:, a0:a1], q, kall[sl, t4, a0:a1], True, True, *free)
                    got.append((b, ps, t))
                st2[i] = (n, got)

            e_free = [None]
            pt2_free = [None]
            vb_free = [None, None]

            def soft2(i):
                n, got = st2[i]
                sm = mvec[:, 40 + (i % 2) * 8:48 + (i % 2) * 8]
                ends = []
                for p, (b, ps, t) in enumerate(got):
                    nm, su = sm[:, 2 * p:2 * p + 1], sm[:, 2 * p + 1:2 * p + 2]
                    a = rmax(nm, ps[:, 0:n], t)
                    a = ts(dve, nm, nm, -0.125, None, ALU.mult, None, a)
                    a = af(e_buf[p][:, 0:n], ps[:, 0:n], ACT.Exp, a, e_free[0], dve.last(), scale=0.125, bias=nm,
                           accum=su)
                    release2(b, a)
                    a = recip(su, su, a)
                    ends.append(a)
                r1 = sm[:, 3:4]
                a = tt(dve, r1, r1, nlam, ALU.mult, *ends)
                c = ts(dve, e_buf[1][:, 0:n], e_buf[1][:, 0:n], r1, None, ALU.mult, None, a)
                c = stt(e_buf[0][:, 0:n], e_buf[0][:, 0:n], sm[:, 1:2], e_buf[1][:, 0:n], ALU.mult, ALU.add, c)
                st2[i] = (n, c)

            def out2(i):
                kind, qb, t4 = jobs2[i]
                n, c = st2.pop(i)
                nt = n // 128
                b, ps, free = bank2()
                for j in range(nt):
                    t = flip(ps[:, j * 128:j * 128 + 128], e_buf[0][:, j * 128:j * 128 + 128], c, *free)
                e_free[0] = t
                c = af(p_t[:, 0:nt, :].rearrange("p j q -> p (j q)"), ps[:, 0:n], ACT.Copy, t, pt2_free[0])
                release2(b, c)
                if t4 == 0:
                    held_out[(kind, qb)] = bank_held()
                ob, po_, free = held_out[(kind, qb)]
                for j in range(nt):
                    t = mm(po_[:, t4 * 128:t4 * 128 + 128], vall[:, j, t4 * 128:t4 * 128 + 128], p_t[:, j, :],
                           j == 0, j == nt - 1, c, *free)
                pt2_free[0] = t
                if t4 == 3:
                    s0 = sq[:, 0, :]
                    a = af(s0, po_, ACT.Square, t, dve.last(), act.last())
                    b1, p1, free = b, ps, bank_free[b]
                    m_ = mm(p1[:, 0:512], ones[:, :], s0, True, True, a, *free)
                    r = sq[:, 1, :]
                    a0, a1 = rsqrt(r, p1[:, 0:512], 1.0 / 128, m_, dve.last())
                    release2(b1, a0)
                    a = stt(s0, po_, gs, r, ALU.mult, ALU.mult, a1)
                    release(ob, a)
                    dst = hc2 if kind else hh
                    sv = s0.rearrange("p (t q) -> p t q", t=4)
                    split_act(dst[:, 0, 4:8, qb * 128:qb * 128 + 128], dst[:, 1, 4:8, qb * 128:qb * 128 + 128],
                              sv, a)

            scores2(0)
            for i in range(len(jobs2)):
                soft2(i)
                if i + 1 < len(jobs2):
                    scores2(i + 1)
                out2(i)
            rotating[0] = 8
            pre = barrier()
            streams = [(rh, T)] + ([] if last else [(rc, TC)])
            for half in range(2):
                evs = [residual(xT, T, 2, 0)(half * 4), residual(ctx2, TC, 2, 1)(half * 4)]
                tiles_of(4, streams, lambda m, j, ps, t, b: evs[j](m, j, ps, t, b))
            t_n = [norm_mod(xT, T, lambda k: col(A2, k), lambda k: mod[:, 24 + k, 0:1], hh)]
            if not last:
                t_n.append(norm_mod(ctx2, TC, lambda k: col(A2c, k), lambda k: mod[:, 24 + k, 1:2], hc2))
            st_list = [(hh, g2, xT, T, 0)] + ([] if last else [(hc2, gc2, ctx2, TC, 1)])
            mlp(st_list, t_n)
            barrier()

        t_rs = rms_rows(xT, T)
        for k in range(KT):
            a = stt(xT[:, k, :], xT[:, k, :], Q2("gfin", 0)[:, k:k + 1], rs[:, :], ALU.mult, ALU.mult, t_rs)
        d_out = Dma(sem("d_out"), "d_out")
        t = d_out.start(sp, out, xT[:, :, :], a)
        sp.wait(t)

        with nc.Block() as block:
            @block.tensor
            def _(e):
                for f in pe.ops:
                    f(e)

            @block.vector
            def _(e):
                for f in dve.ops:
                    f(e)

            @block.scalar
            def _(e):
                for f in act.ops:
                    f(e)

            @block.gpsimd
            def _(e):
                for f in pool.ops:
                    f(e)

            @block.sync
            def _(e):
                for f in sp.ops:
                    f(e)


def constants():
    c = {}
    i, j = np.arange(P)[:, None], np.arange(P)[None, :]
    same = i // 64 == j // 64
    c["ident"] = i == j
    c["bd"] = same
    for name, h in (("perm1", 16), ("perm2", 32)):
        c[name] = np.where((j % (2 * h) < h) & (i == j + h), -1.0, 0.0) + ((j % (2 * h) >= h) & (i == j - h))
    c["trif"] = same & (i <= j)
    c["trib"] = same & (i >= j)
    c["mprev"] = np.where(j >= i, 0.0, NEG)
    c["mnext"] = np.where(j <= i, 0.0, NEG)
    r, v = np.arange(P)[:, None] % 64, np.arange(64)[None, :]
    c["i64"] = r == v
    c["mstrict"] = np.concatenate([np.where(r > v, 0.0, NEG), np.where(r < v, 0.0, NEG)], 1)
    c["mincl"] = np.concatenate([np.where(v >= r, 0.0, NEG), np.where(v <= r, 0.0, NEG)], 1)
    c["lvl"] = np.concatenate([(r // (2 * s) == v // (2 * s)) & (r // s != v // s) for s in (1, 2, 4, 8, 16, 32)], 1)
    sel = np.zeros((P, 2, 2, 2, 4))
    for p in range(2):
        for d in range(2):
            for pr in range(4):
                for b in range(2):
                    sel[32 * b + 8 * d + 2 * pr + p, p, b, d, pr] = 1.0
    c["sel"] = sel.reshape(P, 32)
    edge = np.ones((4, 16))
    for g, w in enumerate((2, 4, 8, 16)):
        for t in range(8):
            edge[g, t] = w / min(w, t + w // 2)
            edge[g, 15 - t] = w / min(w, t + 1 + w // 2)
    c["edge"] = np.broadcast_to(edge.reshape(1, 64), (P, 64))
    small = np.concatenate([np.asarray(c[n], np.float32) for n, _ in CONSTS], 1)
    assert small.shape == (P, CW)
    t = np.arange(T)
    freqs = (10000.0 ** (-np.arange(16) / 16.0)).astype(np.float32).astype(np.float64)
    row, column = t // 64, t % 64
    m = np.arange(64)
    ang1 = np.where((m < 32)[:, None], row[None, :], column[None, :]) * freqs[m % 16][:, None]
    ang2 = np.where((m % 32 < 16)[:, None], row[None, :], column[None, :]) * freqs[m % 16][:, None]
    ropes = [np.stack([np.cos(np.tile(a, (2, 1))), np.sin(np.tile(a, (2, 1)))], 1).astype(np.float32)
             for a in (ang1, ang2)]
    return small, np.concatenate([np.asarray(c[n], np.float32) for n, _ in CONSTS2], 1), ropes[0], ropes[1]


def kernel(**inputs):
    import concourse.bacc as bacc
    from concourse.bass_utils import run_bass_kernel_spmd

    x = {k: np.asarray(v) for k, v in inputs.items()}

    def tiles(w, cols=512):
        k, n = w.shape
        return np.ascontiguousarray(w.reshape(k // P, P, n // cols, cols).transpose(2, 1, 0, 3)).reshape(
            n // cols, P, -1)

    def fm(a):
        return np.ascontiguousarray(a.T.reshape(KT, P, -1).transpose(1, 0, 2))

    def vec(v):
        return v.reshape(-1, P).T

    A = {}
    A["consts"], A["consts2"], A["rope1"], A["rope2"] = constants()
    A["xT"], A["ctxT"], A["ctxT2"] = fm(x["x"][0]), fm(x["ctx"][0]), fm(x["ctx_2"][0])
    w = x["w_in"][0]
    cut = np.cumsum([0, 512, 128, 128, 512, 512, 512, 512, 16, 16, 1024, 1024])
    aq, ak, av, dq, dk, dv, dz, da, db, ga, gd = (w[:, a:b] for a, b in zip(cut[:-1], cut[1:]))
    order = np.array([0, 4, 1, 5, 2, 6, 3, 7])
    aq = aq.reshape(1024, 8, 64)[:, order].reshape(1024, 512)
    A["w_kv"] = tiles(np.concatenate([ak, av], 1), 256)[0]
    A["w_ab"] = tiles(np.concatenate([da, np.zeros((1024, 16), w.dtype), db], 1), 48)[0].reshape(P, KT, 48)
    A["w_1"] = np.concatenate([tiles(m) for m in (aq, dk, dv, dq, dz)], 0)
    br = np.concatenate([x["w_br_attn"][0].reshape(8, 64, 1024)[order].reshape(512, 1024), x["w_br_dn"][0]], 0)
    A["w_mg"] = np.concatenate([tiles(np.concatenate([m[:, i * P:i * P + P] for m in (ga, gd, br)], 1), 384)
                                for i in range(8)], 0)
    A["w_out"] = tiles(x["w_out"][0])
    A["w_ada"] = tiles(x["w_ada"][0])

    def mlp_tiles(w1, w2):
        return tiles(w1), np.concatenate([tiles(w2[q * 1024:(q + 1) * 1024]) for q in range(4)], 0)

    A["w_mlp1"], A["w_mlp2"] = mlp_tiles(x["w_mlp1"][0], x["w_mlp2"][0])

    def rows(v, at=0):
        out = np.zeros((P, 1), v.dtype)
        out[at:at + v.size, 0] = v
        return out

    def cvecs(c, cc):
        return np.stack([vec(c), vec(cc)], 2).reshape(P, 16)

    A["par1"] = np.concatenate([
        cvecs(x["c"][0], x["c_ctx"]), vec(x["b_ada"][0]), vec(x["g_norm1"][0]), vec(x["g_norm2"][0]),
        np.tile(x["q_norm_g"][0], 2)[:, None], np.tile(x["k_norm_g"][0], 2)[:, None],
        np.broadcast_to(x["attn_sink"][0][None], (P, 8)),
        np.concatenate([vec(x["conv_w"][0][t]) for t in range(3)], 1),
        rows(x["a_log"][0].reshape(-1)), rows(x["dt_bias"][0].reshape(-1)),
        np.tile(x["dn_norm_g"][0], 2)[:, None]], 1)
    par2, pools = [], []
    for l in range(2):
        lam = np.concatenate([rows(x[n][l]) for n in ("lam_q1_2", "lam_k1_2", "lam_q2_2", "lam_k2_2")], 1)
        par2.append(np.concatenate([
            cvecs(x["c_2"][0], x["c_ctx_2"]), vec(x["b_ada_2"][l]), vec(x["g_mix_2"][l]), vec(x["g_mlp_2"][l]),
            vec(x["s_pool_2"][l]), x["g_subln_2"][l][:, None], lam,
            vec(x["g_final_2"])], 1))
        A[f"w_ada2_{l}"] = tiles(x["w_ada_2"][l])
        A[f"w_in2_{l}"] = tiles(x["w_in_2"][l])
        A[f"w_out2_{l}"] = tiles(x["w_out_2"][l])
        A[f"w_m1_{l}"], A[f"w_m2_{l}"] = mlp_tiles(x["w_mlp1_2"][l], x["w_mlp2_2"][l])
    A["par2"] = np.stack(par2, 1)
    A["w_pool"] = np.ascontiguousarray(x["w_pool_2"].transpose(0, 2, 1, 3))

    nc = bacc.Bacc("TRN2", target_bir_lowering=False, num_devices=1)
    arrays, I = {}, {}
    for name, a in A.items():
        a = np.ascontiguousarray(a)
        arrays[f"in_{name}"] = a
        I[name] = nc.dram_tensor(f"in_{name}", a.shape, F32, kind="ExternalInput").ap()
    out = nc.dram_tensor("out_x", (P, KT, T), F32, kind="ExternalOutput").ap()
    build(nc, I, out)
    got = run_bass_kernel_spmd(nc, [arrays], core_ids=[0]).results[0]["out_x"]
    return np.ascontiguousarray(got.transpose(2, 1, 0)).reshape(1, T, 1024)
```

```python
from contextlib import ExitStack

import numpy as np

import concourse.bass as bass
from concourse import mybir

F32 = mybir.dt.float32
F32R = mybir.dt.float32r
ALU = mybir.AluOpType
ACT = mybir.ActivationFunctionType
AXX = mybir.AxisListType.X

P = 128
KT = 8
T = 512
TC = 256
EPS = 1e-6
SET_EXP_LN = 6
SET_SIGMOID = 2
NEG = -1e30

CONSTS = (("ident", 128), ("bd", 128), ("perm1", 128), ("trif", 128), ("trib", 128),
          ("mprev", 128), ("mnext", 128), ("i64", 64), ("mstrict", 128), ("mincl", 128), ("lvl", 6 * 64),
          ("sel", 32))
CONSTS2 = (("perm2", 128), ("edge", 64))
CW = sum(w for _, w in CONSTS)
CW2 = sum(w for _, w in CONSTS2)
PAR1 = (("c", 16), ("bada", 48), ("gn1", 8), ("gn2", 8), ("qg", 1), ("kg", 1), ("sink", 8), ("convw", 36),
        ("alog", 1), ("dtb", 1), ("dng", 1))
PAR2 = (("c", 16), ("bada", 48), ("gmix", 8), ("gmlp", 8), ("spool", 4), ("gsub", 1), ("lam", 4), ("gfin", 8))
PW1 = sum(w for _, w in PAR1)
PW2 = sum(w for _, w in PAR2)


def offsets(fields):
    at, out = 0, {}
    for n, w in fields:
        out[n] = (at, w)
        at += w
    return out


class Engine:

    def __init__(self, name, sem, chained=True):
        self.name, self.sem, self.count, self.ops, self.seen = name, sem, 0, [], {}
        self.chained = chained

    def wait(self, *tokens):
        for t in tokens:
            if t is None:
                continue
            sem, value, key = t
            if self.seen.get(key, 0) < value:
                self.seen[key] = value
                self.ops.append(lambda e, s=sem, v=value: e.wait_ge(s, v))

    def __call__(self, fn, *after):
        self.wait(*after)
        if self.chained and self.count:
            self.wait(self.last())
        self.count += 1
        self.ops.append(lambda e: fn(e).then_inc(self.sem, 1))
        return (self.sem, self.count, self.name)

    def silent(self, fn, *after):
        self.wait(*after)
        self.ops.append(lambda e: fn(e))

    def last(self):
        return (self.sem, self.count, self.name)


class Dma:

    def __init__(self, sem, key):
        self.sem, self.key, self.n = sem, key, 0

    def start(self, q, out, in_, *after):
        q.wait(*after)
        self.n += 16
        q.ops.append(lambda e: e.dma_start(out, in_).then_inc(self.sem, 16))
        return (self.sem, self.n, self.key)


def build(nc, I, out):
    ctx = ExitStack()
    with ctx:
        def sem(name):
            return ctx.enter_context(nc.semaphore(name))

        pe = Engine("pe", sem("s_pe"), chained=False)
        dve = Engine("dve", sem("s_dve"))
        act = Engine("act", sem("s_act"))
        pool = Engine("pool", sem("s_pool"))
        sp = Engine("sp", sem("s_sp"))
        engines = (pe, dve, act, pool)

        def sb(name, shape, dt=F32, stack=ctx):
            return stack.enter_context(nc.sbuf_tensor(name, shape, dt))

        RAWN, WSN = 3, 3
        raw = sb("raw", [P, RAWN, 4096])
        ws = sb("ws", [P, WSN, 2, 1024], F32R)
        hh = sb("hh", [P, 2, KT, T], F32R)
        xT = sb("xT", [P, KT, T])
        cst = sb("cst", [P, CW])
        mods = sb("mods", [P, 3, 48, 2])
        par1 = sb("par1", [P, PW1])
        par2 = sb("par2", [P, 2, PW2])
        mvec = sb("mvec", [P, 64])
        ones = sb("ones", [P, P])
        rs = sb("rs", [P, T])
        sq = sb("sq", [P, 2, T])
        mi = sb("mi", [P, 8])
        REST = 18432

        def region(names):
            st = ExitStack()
            got = [sb(n, s, dt, st) for n, s, dt in names]
            st.close()
            return got

        ar, = region([("ar", [P, REST], F32)])
        hc1, = region([("hc1", [P, 2, KT, TC], F32R)])
        gg, yy = region([("gg", [P, 2, KT, T], F32R), ("yy", [P, 2, KT, T], F32R)])
        ctx2, hc2, ar2 = region([("ctx2", [P, KT, TC], F32), ("hc2", [P, 2, KT, TC], F32R),
                                 ("ar2", [P, REST - 6144], F32)])
        _, _, g2, gc2 = region([("pad_a", [P, KT, TC], F32), ("pad_b", [P, 2, KT, TC], F32R),
                                ("g2", [P, 2, KT, T], F32R), ("gc2", [P, 2, KT, TC], F32R)])

        psum = [ctx.enter_context(nc.psum_tensor(f"ps{i}", [P, 1024], F32)) for i in range(4)]
        bank_free = [[] for _ in range(8)]
        bank_at = [0]

        rotating = [8]
        held = [False] * 8

        def bank():
            for _ in range(8):
                b = bank_at[0] % rotating[0]
                bank_at[0] = b + 1
                if not held[b]:
                    held[b] = True
                    return b, psum[b // 2][:, (b % 2) * 512:(b % 2) * 512 + 512], bank_free[b]
            raise ValueError("no bank is free")

        def bank2():
            for _ in range(8):
                b = (bank_at[0] + bank_at[0] % 2) % rotating[0]
                bank_at[0] = b + 2
                if not held[b] and not held[b + 1]:
                    held[b] = held[b + 1] = True
                    return b, psum[b // 2], bank_free[b] + bank_free[b + 1]
            raise ValueError("no pair of banks is free")

        def bank_held():
            b = 7 if held[6] else 6
            assert not held[b]
            held[b] = True
            return b, psum[3][:, (b - 6) * 512:(b - 6) * 512 + 512], bank_free[b]

        def release(b, *tokens):
            bank_free[b] = list(tokens)
            held[b] = False

        def release2(b, *tokens):
            bank_free[b] = bank_free[b + 1] = list(tokens)
            held[b] = held[b + 1] = False

        co, co2 = offsets(CONSTS), offsets(CONSTS2)

        def C(name):
            if name in co2:
                a, w = co2[name]
                a += CW - CW2
            else:
                a, w = co[name]
            return cst[:, a:a + w]

        d_small = [Dma(sem(f"d_small{i}"), f"d_small{i}") for i in range(8)]
        d_raw = [Dma(sem(f"d_raw{i}"), f"d_raw{i}") for i in range(RAWN)]
        t_par = d_small[2].start(pool, par1[:, :], I["par1"])
        t_x = d_small[1].start(pool, xT[:, :, :], I["xT"])

        raw_free = [[] for _ in range(RAWN)]
        raw_order = list(range(RAWN))
        raw_busy = [False] * RAWN

        def place():
            k = next(k for k in raw_order if not raw_busy[k])
            raw_order.remove(k)
            raw_order.append(k)
            raw_busy[k] = True

            def done(*tokens):
                raw_free[k] = list(tokens)
                raw_busy[k] = False
            return k, done

        def load(src, w):
            k, done = place()
            t = d_raw[k].start(sp, raw[:, k, 0:w], src, *raw_free[k])
            return raw[:, k, 0:w], t, done

        def reserve():
            k, done = place()
            return raw[:, k, :], raw_free[k], done

        plan = []
        ready = []
        ws_n = [0]
        ws_free = [None] * WSN
        cur = [None]

        def split_next():
            if cur[0] is None:
                src, kt, cols, pk, pc = plan.pop(0)
                w, t_w, done = load(src, kt * cols)
                wv = w.rearrange("p (k c) -> p k c", k=kt)
                pieces = [wv[:, k:k + pk, c:c + pc] for k in range(0, kt, pk) for c in range(0, cols, pc)]
                cur[0] = [pieces, t_w, done, pk, pc]
            pieces, t_w, done, pk, pc = cur[0]
            w = pieces.pop(0)
            s = ws_n[0] % WSN
            ws_n[0] += 1
            hi = ws[:, s, 0, 0:pk * pc].rearrange("p (k c) -> p k c", k=pk)
            lo = ws[:, s, 1, 0:pk * pc].rearrange("p (k c) -> p k c", k=pk)
            t_hi = act(lambda e: e.activation(hi, w, ACT.Copy), t_w, ws_free[s])
            t_lo = dve(lambda e: e.tensor_tensor(lo, w, hi.bitcast(F32), ALU.subtract), t_hi, t_w, ws_free[s])
            if not pieces:
                done(t_hi, t_lo)
                cur[0] = None
            ready.append((s, hi, lo, t_hi, t_lo))

        def coming(*blocks, kt=KT, cols=512, pk=KT, pc=128):
            plan.extend((src, kt, cols, pk, pc) for src in blocks)

        def ahead():
            while len(ready) < WSN and (cur[0] is not None or plan):
                split_next()

        def piece():
            ahead()
            return ready.pop(0)

        pending = []

        def later(stages):
            for g in list(pending):
                if next(g, "end") == "end":
                    pending.remove(g)
            if stages is not None:
                pending.append(stages)

        def flush():
            while pending:
                later(None)

        def mm(o, l, r, start, stop, *after):
            return pe(lambda e: e.matmul(o, l, r, start=start, stop=stop), *after)

        def mmq(o, l, r, start, stop, *after):
            pe.silent(lambda e: e.matmul(o, l, r, start=start, stop=stop), *after)

        def product(o, lhs, rhs, kt, *after, by_k=None):
            pe.wait(*after)
            n, total = 0, 3 * kt
            t = None
            for k in range(kt):
                (lh, ll), (rh, rl) = lhs(k), rhs(k)
                if by_k is not None:
                    pe.wait(*by_k[k])
                for a, b in ((lh, rh), (lh, rl), (ll, rh)):
                    f = mm if n == total - 1 else mmq
                    t = f(o, a, b, n == 0, n == total - 1)
                    n += 1
            return t

        def act_set(n):
            act.ops.append(lambda e: e.add_instruction(mybir.InstLoadActFuncSet(
                name=nc.get_next_instruction_name(), act_func_set_id=n,
                engine=mybir.EngineType.Activation, ins=[], outs=[])))

        def tt(eng, o, a, b, op, *after):
            return eng(lambda e: e.tensor_tensor(o, a, b, op), *after)

        def ts(eng, o, a, s1, s2, op0, op1, *after):
            if s2 is None:
                return eng(lambda e: e.tensor_scalar(o, a, s1, None, op0), *after)
            return eng(lambda e: e.tensor_scalar(o, a, s1, s2, op0, op1), *after)

        def stt(o, a, s, b, op0, op1, *after):
            return dve(lambda e: e.scalar_tensor_tensor(o, a, s, b, op0, op1), *after)

        def af(o, i, f, *after, scale=1.0, bias=None, accum=None):
            kw = {}
            if bias is not None:
                kw["bias"] = bias
            if accum is not None:
                kw["accum_out"] = accum
            return act(lambda e: e.activation(o, i, f, scale=scale, **kw), *after)

        def copy(eng, o, i, *after):
            return eng(lambda e: e.tensor_copy(o, i), *after)

        def fill(o, v, *after):
            return pool(lambda e: e.memset(o, v), *after)

        def rmax(o, i, *after):
            return dve(lambda e: e.reduce_max(o, i, AXX), *after)

        def rsum(o, i, *after):
            return dve(lambda e: e.reduce_sum(o, i, AXX), *after)

        def recip(o, i, *after):
            return dve(lambda e: e.reciprocal(o, i), *after)

        def flip(o, i, *after):
            return pe(lambda e: e.transpose(o, i, C("ident")), *after)

        def barrier():
            flush()
            now = [e.last() for e in engines]
            for e in engines:
                e.wait(*[t for t in now if t[2] != e.name or e is not pe])
            assert not any(held)
            for i in range(8):
                bank_free[i] = list(now)
            return now

        act_set(SET_EXP_LN)
        t_ones = pool(lambda e: e.memset(ones[:, :], 1.0))
        t_mi = pool(lambda e: e.memset(mi[:, 0:1], EPS))
        eps = mi[:, 0:1]

        def split_act(hi, lo, src, *after):
            a = af(hi, src, ACT.Copy, *after)
            b = tt(dve, lo, src, hi.bitcast(F32), ALU.subtract, a, *after)
            return a, b

        def rsqrt(o, src, scale, *after):
            a = af(o, src, ACT.Ln, t_mi, *after, scale=scale, bias=eps[0:o.shape[0], :])
            return a, af(o, o, ACT.Exp, a, scale=-0.5)

        class Stats:

            def __init__(self, n, bufs):
                self.n, self.bufs, self.prev, self.k = n, bufs, [None, None], 0
                self.b, self.ps, self.free = bank()

            def tile(self, x, *after):
                i = self.k
                self.k += 1
                a = af(self.bufs[i % 2], x, ACT.Square, self.prev[i % 2], *after)
                yield
                self.prev[i % 2] = mm(self.ps[:, 0:self.n], ones[:, :], self.bufs[i % 2], i == 0, i == KT - 1, a,
                                      t_ones, *self.free)

            def root(self, o, *after):
                a, t = rsqrt(o, self.ps[:, 0:self.n], 1.0 / 1024, self.prev[1], *after)
                release(self.b, a)
                return t

        def rms_rows(x, n, o, *after):
            act.wait(dve.last(), pe.last(), pool.last())
            st_ = Stats(n, [sq[:, i, 0:n] for i in range(2)])
            for k in range(KT):
                for _ in st_.tile(x[:, k, :], *after):
                    pass
            return st_.root(o)

        def norm_mod(x, n, av, bv, dst, r, t_rs, more, *after):
            bufs = [sq[:, 0, 0:n], sq[:, 1, 0:n], more[:, 0:n], more[:, 512:512 + n]]
            hist = [[pe.last(), dve.last(), act.last()]] * 4
            toks = []
            for k in range(KT):
                s = bufs[k % 4]
                hi, lo = dst[:, 0, k, :], dst[:, 1, k, :]
                y = tt(pool, s, x[:, k, :], r, ALU.mult, t_rs, *hist[k % 4])
                a = af(hi, s, ACT.Identity, y, *after, scale=av(k), bias=bv(k))
                b = ts(dve, s, s, av(k), bv(k), ALU.mult, ALU.add, a)
                c = tt(dve, lo, s, hi.bitcast(F32), ALU.subtract, b)
                hist[k % 4] = [c]
                toks.append([a, c])
            return toks

        def pair(tile, k, sl=slice(None)):
            return tile[:, 0, k, sl], tile[:, 1, k, sl]

        c32 = ar[:, 16128:16384].rearrange("p (k j) -> p k j", j=32)

        def ada_start(cv, t_par, after):
            a = fill(c32.rearrange("p k j -> p (k j)"), 0.0, *after)
            u = mvec[:, 40:56].rearrange("p (k j) -> p k j", j=2)
            a1 = af(u, cv, ACT.Abs, t_par, *after)
            a1 = af(u, u, ACT.Exp, a1, scale=-1.0)
            a1 = af(u, u, ACT.Ln, a1, bias=1.0)
            a1 = stt(u, cv, 0.0, u, ALU.min, ALU.subtract, a1)
            a1 = af(u, u, ACT.Exp, a1)
            return tt(dve, c32[:, :, 0:2], cv, u, ALU.mult, a, a1)

        def ada_block(srcs, blk, dst, bias, t_c):
            w, t_w, done = load(srcs[blk], 4096)
            yield
            wv = w.rearrange("p (k c) -> p k c", k=KT)
            b, ps, free = bank()
            for k in range(KT):
                g = (k % 4) * 32
                f = mm if k == KT - 1 else mmq
                t = f(ps[g:g + 32, :], c32[:, k, :], wv[:, k, :], k < 4, k >= 4, t_c, t_w, *free)
            done(t)
            yield
            r = ada_row
            a = af(r, ps, ACT.Copy, t, ada_last[0])
            release(b, a)
            yield
            b, ps, free = bank()
            for m in range(4):
                t = flip(ps[:, m * 128:m * 128 + 128], r[:, m * 128:m * 128 + 128], a, t_cst, *free)
            ada_last[0] = t
            yield
            o = dst[:, 4 * blk:4 * blk + 4, :]
            a = rsum(o, ps.rearrange("p (m g j) -> p m j g", m=4, g=4)[:, :, 0:2, :], t)
            release(b, a)
            bb = bias[:, 4 * blk:4 * blk + 4].rearrange("p (m o) -> p m o", o=1).to_broadcast([P, 4, 2])
            ada_done[0] = tt(dve, o, o, bb, ALU.add, a)
            yield

        ada_row = ar[:, 12288:12800]
        ada_last = [None]
        ada_done = [None]

        def gain(o, part, j, g, t_mod):
            return stt(o, mod[:, part * 8:part * 8 + 8, j], 1.0, g, ALU.add, ALU.mult, t_mod)

        po = offsets(PAR1)
        mod = mods[:, 0, :, :]

        def Q(name):
            a, w = po[name]
            return par1[:, a:a + w]

        YA = REST - 2048
        cx = ar[:, YA:YA + 2048].rearrange("p (k n) -> p k n", k=KT)
        t_cx = d_small[3].start(pool, cx, I["ctxT"])
        t_cst = d_small[0].start(pool, cst[:, :], I["consts"])
        t_par2 = d_small[6].start(pool, par2[:, :, :], I["par2"])
        cs1 = ar[:, 14592:15616].rearrange("p (k n) -> p k n", k=2)
        t_cs1 = d_small[4].start(pool, cs1, I["rope1"])
        po2 = offsets(PAR2)

        def Q2(name, layer):
            a, w = po2[name]
            return par2[:, layer, a:a + w]

        rsc = ar[:, 12800:13056]
        c8 = lambda v: v.rearrange("p (k j) -> p k j", j=2)
        t_c = ada_start(c8(Q("c")), t_par, [])
        for blk in range(4):
            later(ada_block(I["w_ada"], blk, mod, Q("bada"), t_c))
            if blk == 3:
                later(None)
                t_rsx = rms_rows(xT, T, rs[:, :], t_x)
                t_rsc = rms_rows(cx, TC, rsc, t_cx)
        flush()
        t_mod = ada_done[0]
        A1, A1c, A2 = mvec[:, 0:8], mvec[:, 8:16], mvec[:, 16:24]
        t_a1 = gain(A1, 1, 0, Q("gn1"), t_mod)
        t_a1c = gain(A1c, 1, 1, Q("gn1"), t_mod)
        col = lambda v, k: v[:, k:k + 1]
        coming(I["w_kv"], cols=256)
        coming(I["w_ab"], cols=48, pc=48)
        coming(*(I["w_1"][i] for i in range(4)))
        ahead()
        t_h = norm_mod(xT, T, lambda k: col(A1, k), lambda k: mod[:, k, 0:1], hh, rs[:, :], t_rsx,
                       ar[:, 10240:11264], t_a1, t_mod)
        t_hc = norm_mod(cx, TC, lambda k: col(A1c, k), lambda k: mod[:, k, 1:2], hc1, rsc, t_rsc, ar[:, 9216:10240],
                        t_a1c, t_mod)

        def part(at, k, n):
            return ar[:, at:at + k * n].rearrange("p (k n) -> p k n", k=k)

        kT, kTc = part(4096, 4, T), part(6144, 4, TC)
        qT = part(7168, 4, T)
        vT, vTc = part(9216, 4, T), part(11264, 4, TC)
        abr = ar[:, 12288:13056]
        ka, kac = ar[:, 13056:13568], ar[:, 13568:13824]
        va = part(13824, 6, 128)
        ya = qa = part(YA, 4, T)

        def conv(ps, n, j, dst, t, b):
            w = Q("convw")
            a = af(dst, ps[:, 0:n], ACT.Identity, t, t_par, scale=w[:, 12 + j:13 + j])
            a = stt(dst[:, 1:n], ps[:, 0:n - 1], w[:, j:j + 1], dst[:, 1:n], ALU.mult, ALU.add, a)
            a = stt(dst[:, 0:n - 1], ps[:, 1:n], w[:, 24 + j:25 + j], dst[:, 0:n - 1], ALU.mult, ALU.add, a)
            release(b, a)
            return a

        def head_rope(ps, n, g, dst, t, b, roped, tables, t_tab, perm, end=None):
            a = af(dst, ps[:, 0:n], ACT.Copy, t)
            if g is not None:
                s = sq[:, 0, 0:n]
                a2 = af(s, ps[:, 0:n], ACT.Square, t, pe.last(), dve.last())
                release(b, a2)
                b1, p1, free = bank()
                m = mm(p1[:, 0:n], C("bd"), s, True, True, a2, t_cst, *free)
                yield
                r = sq[:, 1, 0:n]
                e0, e1 = rsqrt(r, p1[:, 0:n], 1.0 / 64, m, dve.last())
                release(b1, e0)
                a = stt(dst, dst, g, r, ALU.mult, ALU.mult, a, e1)
            else:
                release(b, a)
            if roped:
                yield
                b2, p2, free = bank()
                m = mm(p2[:, 0:n], C(perm), dst, True, True, a, t_cst, *free)
                yield
                r = sq[:, 1, 0:n]
                a1 = tt(dve, r, p2[:, 0:n], tables[:, 1, 0:n], ALU.mult, m, t_tab, act.last())
                release(b2, a1)
                a2 = tt(dve, dst, dst, tables[:, 0, 0:n], ALU.mult, a, m, t_tab)
                a = tt(dve, dst, dst, r, ALU.add, a1, a2)
            if end is not None:
                end[0] = a

        s, hi, lo, t_hi, t_lo = piece()
        lw = lambda k, hi=hi, lo=lo: (hi[:, k, :], lo[:, k, :])
        bk, pk, free = bank()
        tk = product(pk[:, 0:T], lw, lambda k: pair(hh, k), KT, t_hi, t_lo, *free, by_k=t_h)
        bkc, pkc, free = bank()
        tkc = product(pkc[:, 0:TC], lw, lambda k: pair(hc1, k), KT, *free, by_k=t_hc)
        ws_free[s] = tkc
        t_ka, t_kac = [None], [None]
        later(head_rope(pk, T, Q("kg"), ka, tk, bk, True, cs1, t_cs1, "perm1", t_ka))
        later(head_rope(pkc, TC, Q("kg"), kac, tkc, bkc, False, None, None, None, t_kac))
        s, hi, lo, t_hi, t_lo = piece()
        rw = lambda k, hi=hi, lo=lo: (hi[:, k, :], lo[:, k, :])
        b, ps, free = bank()
        for i in range(4):
            t = product(ps[:, i * 128:i * 128 + 128], lambda k: pair(hh, k, slice(i * 128, i * 128 + 128)), rw, KT,
                        t_hi, t_lo, *free)
        bc, psc, free = bank()
        for i in range(2):
            t2 = product(psc[:, i * 128:i * 128 + 128], lambda k: pair(hc1, k, slice(i * 128, i * 128 + 128)), rw,
                         KT, *free)
        ws_free[s] = t2
        t_va = af(va[:, 0:4, :].rearrange("p t n -> p (t n)"), ps[:, :], ACT.Copy, t, *t_hc[-1])
        t_vac = af(va[:, 4:6, :].rearrange("p t n -> p (t n)"), psc[:, 0:TC], ACT.Copy, t2)
        release(b, t_va)
        release(bc, t_vac)
        flush()
        s, hi, lo, t_hi, t_lo = piece()
        for src, n, at in ((hh, T, 0), (hc1, TC, T)):
            b2, ps2, free = bank()
            t = product(ps2[0:48, 0:n], lambda k: (hi[:, k, :], lo[:, k, :]), lambda k: pair(src, k), KT, t_hi, t_lo,
                        *free)
            ws_free[s] = t
            x1 = abr[0:48, 0:768][:, at:at + n]
            x2 = sq[0:48, 0, 0:n]
            a = af(x1, ps2[0:48, 0:n], ACT.Identity, t, t_par, bias=Q("dtb")[0:48, :])
            release(b2, a)
            a = af(x2, x1, ACT.Abs, a, dve.last())
            a = af(x2, x2, ACT.Exp, a, scale=-1.0)
            a = af(x2, x2, ACT.Ln, a, bias=1.0)
            if not at:
                ea = mi[0:32, 1:2]
                t_ea = af(ea, Q("alog")[0:32, :], ACT.Exp, t_par)
                t_ea = ts(dve, ea, ea, -1.0, None, ALU.mult, None, t_ea)
            c1 = stt(x1[0:32, :], x1[0:32, :], 0.0, x2[0:32, :], ALU.max, ALU.add, a)
            c1 = ts(dve, x1[0:32, :], x1[0:32, :], ea, None, ALU.mult, None, c1, t_ea)
            c2 = stt(x1[32:48, :], x1[32:48, :], 0.0, x2[32:48, :], ALU.min, ALU.subtract, a)
            c2 = af(x1[32:48, :], x1[32:48, :], ACT.Exp, c2)
        t_ab = [c1, c2]

        def tiles_of(n, streams, evac, pre=(), kt=KT, by_k=None):
            for m in range(n):
                s, hi, lo, t_hi, t_lo = piece()
                for j, (rhs, w) in enumerate(streams):
                    b, ps, free = bank()
                    t = product(ps[:, 0:w], lambda k: (hi[:, k, :], lo[:, k, :]), rhs, kt, t_hi, t_lo, *pre, *free,
                                by_k=by_k[j] if by_k else None)
                    if j == len(streams) - 1:
                        ws_free[s] = t
                    later(evac(m, j, ps, t, b))

        rh = lambda k: pair(hh, k)
        rc1 = lambda k: pair(hc1, k)

        def ev_q(m, j, ps, t, b):
            return head_rope(ps, T, Q("qg"), qa[:, m, :], t, b, True, cs1, t_cs1, "perm1")
        tiles_of(4, [(rh, T)], ev_q)

        def conv_ev(dst, dstc, base):
            def ev(m, j, ps, t, b):
                if j == 0:
                    conv(ps, T, base + m, dst[:, m, :], t, b)
                else:
                    conv(ps, TC, base + m, dstc[:, m, :], t, b)
            return ev
        tiles_of(4, [(rh, T), (rc1, TC)], conv_ev(kT, kTc, 4))
        tiles_of(4, [(rh, T), (rc1, TC)], conv_ev(vT, vTc, 8))
        tiles_of(4, [(rh, T)], conv_ev(qT, None, 0))

        barrier()
        pbuf = [ar[:, i * 640:(i + 1) * 640] for i in range(2)]
        ptb = [ar[:, 1280 + i * 640:1280 + (i + 1) * 640].rearrange("p (j q) -> p j q", j=5) for i in range(2)]
        small = mvec[:, 24:40]
        p_free = [None, None]
        pt_free = [None, None]
        items = [(qb, h) for qb in range(4) for h in range(8)]
        st = {}

        def scores(i):
            qb, h = items[i]
            t4, p = h % 4, h // 4
            q = qa[p * 64:p * 64 + 64, t4, qb * 128:qb * 128 + 128]
            b, ps, free = bank2()
            kr = slice(p * 64, p * 64 + 64)
            mm(ps[:, 0:256], q, kac[kr, :], True, True, *free)
            at = 256
            tiles = []
            for kb in range(max(0, qb - 1), min(4, qb + 2)):
                o_ = ps[:, at:at + 128]
                tiles.append(kb)
                masked = kb != qb
                t = mm(o_, q, ka[kr, kb * 128:kb * 128 + 128], True, not masked)
                if masked:
                    t = mm(o_, C("ident"), C("mprev" if kb < qb else "mnext"), False, True)
                at += 128
            st[i] = (b, ps, at, tiles, t)

        def soft(i):
            qb, h = items[i]
            b, ps, n, tiles, t = st[i]
            sm = small[:, (i % 2) * 8:(i % 2) * 8 + 8]
            mx, nm, su, es, rc = (sm[:, k:k + 1] for k in range(5))
            sink = Q("sink")[:, h:h + 1]
            a = rmax(mx, ps[:, 0:n], t, p_free[i % 2])
            a = ts(dve, nm, mx, 0.125, sink, ALU.mult, ALU.max, a)
            a = ts(dve, nm, nm, -1.0, None, ALU.mult, None, a)
            pb = pbuf[i % 2][:, 0:n]
            a1 = af(pb, ps[:, 0:n], ACT.Exp, a, p_free[i % 2], scale=0.125, bias=nm, accum=su)
            release2(b, a1)
            a2 = af(es, sink, ACT.Exp, a, bias=nm)
            yield
            a = tt(dve, su, su, es, ALU.add, a1, a2)
            a = recip(rc, su, a)
            a = ts(dve, pb, pb, rc, None, ALU.mult, None, a)
            st[i] = (pb, n, tiles, a)

        ops = {}

        def outp(i):
            qb, h = items[i]
            t4, p = h % 4, h // 4
            pb, n, tiles, a = st.pop(i)
            nt = n // 128
            b, ps, free = bank2()
            for j in range(nt):
                t = flip(ps[:, j * 128:j * 128 + 128], pb[:, j * 128:j * 128 + 128], a, *free)
            p_free[i % 2] = t
            pt = ptb[i % 2]
            c = af(pt[:, 0:nt, :].rearrange("p j q -> p (j q)"), ps[:, 0:n], ACT.Copy, t, pt_free[i % 2])
            release2(b, c)
            yield
            if h == 0:
                ops[qb] = bank_held()
            b, ps, free = ops[qb]
            for j in range(nt):
                vt = va[:, 4 + j, p * 64:p * 64 + 64] if j < 2 else va[:, tiles[j - 2], p * 64:p * 64 + 64]
                t = mm(ps[p * 64:p * 64 + 64, t4 * 128:t4 * 128 + 128], vt, pt[:, j, :], j == 0, j == nt - 1,
                       c, t_va, t_vac, *free)
            pt_free[i % 2] = t
            if h == 7:
                c = copy(dve, ya[:, :, qb * 128:qb * 128 + 128], ps.rearrange("p (t q) -> p t q", t=4), t)
                release(b, c)

        rotating[0] = 6
        scores(0)
        softs = [soft(i) for i in range(32)]
        next(softs[0])
        for i in range(33):
            if i < 31:
                scores(i + 1)
            out_ = outp(i - 1) if i else iter(())
            next(out_, None)
            if i < 31:
                next(softs[i + 1])
            if i < 32:
                next(softs[i], None)
            next(out_, None)
        rotating[0] = 8
        barrier()

        act_set(SET_SIGMOID)
        sg = [ar[:, i * 512:(i + 1) * 512] for i in range(4)]
        use = [None] * 4
        jobs = [(kT, m, T) for m in range(4)] + [(vT, m, T) for m in range(4)] + [(qT, m, T) for m in range(4)] \
            + [(kTc, m, TC) for m in range(4)] + [(vTc, m, TC) for m in range(4)]
        for i, (tl, m, n) in enumerate(jobs):
            s = sg[i % 4][:, 0:n]
            a = af(s, tl[:, m, :], ACT.Sigmoid, use[i % 4])
            use[i % 4] = tt(dve, tl[:, m, :], tl[:, m, :], s, ALU.mult, a)
        act_set(SET_EXP_LN)
        t_silu = dve.last()
        jobs = [j for j in jobs if j[0] is not vT and j[0] is not vTc]

        def square(i):
            tl, m, n = jobs[i]
            return af(sg[i % 2][:, 0:n], tl[:, m, :], ACT.Square, t_silu, use[i % 2])

        t_sq = square(0)
        for i, (tl, m, n) in enumerate(jobs):
            r = sg[2 + i % 2][:, 0:n]
            b, ps, free = bank()
            t = mm(ps[:, 0:n], C("bd"), sg[i % 2][:, 0:n], True, True, t_sq, *free)
            if i + 1 < len(jobs):
                t_sq = square(i + 1)
            e0, e1 = rsqrt(r, ps[:, 0:n], 1.0, t)
            release(b, e0)
            if tl is qT:
                use[i % 2] = stt(tl[:, m, :], tl[:, m, :], 0.125, r, ALU.mult, ALU.mult, e1)
            else:
                use[i % 2] = tt(dve, tl[:, m, :], tl[:, m, :], r, ALU.mult, e1)
        barrier()

        ktok = ar[:, 0:3072].rearrange("p (n r v) -> p n r v", n=12, r=4)
        vtok = ar[:, 13056:16128].rearrange("p (n r v) -> p n r v", n=12, r=4)
        for src, srcc, dst in ((kT, kTc, ktok), (vT, vTc, vtok)):
            for n2 in range(6):
                b, ps, free = bank()
                for half in range(2):
                    n = 2 * n2 + half
                    tl, at = (src, n * 64) if n < 8 else (srcc, (n - 8) * 64)
                    for pr in range(4):
                        for p in range(2):
                            sl = slice(p * 64, p * 64 + 64)
                            t = mm(ps[sl, (half * 4 + pr) * 64:(half * 4 + pr) * 64 + 64],
                                   tl[sl, pr, at:at + 64], C("i64")[sl, :], True, True, *free)
                d = dst[:, 2 * n2:2 * n2 + 2, :, :].rearrange("p n r v -> p (n r v)")
                if n2 % 2:
                    c = copy(dve, d, ps, t)
                else:
                    c = af(d, ps, ACT.Copy, t)
                release(b, c)
        barrier()
        gate = rs[:, 0:192].rearrange("p (s b d r) -> p s b d r", s=12, b=2, d=2)
        b, ps, free = bank()
        pg = ps[:, 0:192].rearrange("p (s b d r) -> p s b d r", s=12, b=2, d=2)
        sel = C("sel").rearrange("p (q b d r) -> p q b d r", q=2, b=2, d=2)

        def chunk_of(s, d):
            if s < 4:
                return 8 + (s if d == 0 else 3 - s)
            return s - 4 if d == 0 else 11 - s

        for s in range(12):
            for d in range(2):
                n = chunk_of(s, d)
                at = n * 64
                for p in range(2):
                    sl = slice(p * 64, p * 64 + 64)
                    t = mm(pg[sl, s, :, d, :], abr[0:48, at:at + 64], sel[0:48, p, :, d, :], True, True, *free)
        t = copy(dve, rs[:, 0:192], ps[:, 0:192], t)
        release(b, t)
        t_gate = t
        b, ps, free = bank()
        gcp = ps[:, 0:96].rearrange("p (s d r) -> p s d r", s=12, d=2)
        glp = ps[:, 96:192].rearrange("p (s d r) -> p s d r", s=12, d=2)
        mm(gcp[:, :, 0, :], C("trif"), gate[:, :, 0, 0, :], True, True, t_gate, *free)
        mm(gcp[:, :, 1, :], C("trib"), gate[:, :, 0, 1, :], True, True)
        t = mm(glp, C("bd"), gate[:, :, 0, :, :], True, True)
        gt = rs[:, 192:512]
        Gc = sq[:, 0, 0:96].rearrange("p (s x) -> p s x", s=12)
        eG = sq[:, 0, 96:192].rearrange("p (s x) -> p s x", s=12)
        tail = sq[:, 0, 192:288].rearrange("p (s x) -> p s x", s=12)
        egl = sq[:, 0, 288:384].rearrange("p (s x) -> p s x", s=12)
        beG = sq[:, 0, 384:480].rearrange("p (s x) -> p s x", s=12)
        bet = rs[:, 192:288].rearrange("p (s x) -> p s x", s=12)
        flat = lambda v: v.rearrange("p s x -> p (s x)")
        a = copy(dve, flat(Gc), ps[:, 0:96], t)
        a2 = tt(dve, flat(tail), ps[:, 96:192], flat(Gc), ALU.subtract, a)
        a3 = af(flat(egl), ps[:, 96:192], ACT.Exp, t, a2)
        release(b, a3)
        a4 = af(flat(tail), flat(tail), ACT.Exp, a2)
        a5 = af(flat(eG), flat(Gc), ACT.Exp, a)
        a6 = copy(dve, bet.rearrange("p s (d r) -> p s d r", d=2), gate[:, :, 1, :, :], t_gate)
        a7 = tt(dve, flat(beG), flat(bet), flat(eG), ALU.mult, a5, a6)
        barrier()

        X3 = "p (x v) -> p x v"
        sA, sX, sXt, sV, sIT, sE = (ar[:, 9216 + i * 512:9728 + i * 512].rearrange(X3, x=8) for i in range(6))
        slot, slot_free, slot_done = reserve()
        sKt, sR, sU, sT2 = (slot[:, i * 512:(i + 1) * 512].rearrange(X3, x=8) for i in range(4))
        oacc = slot[:, 2048:4096].rearrange("p (n r v) -> p n r v", n=8, r=4)
        for e in engines:
            e.wait(*slot_free)
        sVb = sq[:, 1, :].rearrange(X3, x=8)
        sS = ar[:, 3072:3584].rearrange(X3, x=8)
        sD = ar[:, 3584:4096].rearrange(X3, x=8)
        t_S = fill(sS.rearrange("p x v -> p (x v)"), 0.0)
        i64b = C("i64").rearrange("p (o v) -> p o v", o=1).to_broadcast([P, 4, 64])
        lv = C("lvl").rearrange("p (l v) -> p l v", l=6)

        def lvb(l):
            return lv[:, l:l + 1, :].to_broadcast([P, 4, 64])

        mst = C("mstrict").rearrange("p (d v) -> p d v", d=2)
        min_ = C("mincl").rearrange("p (d v) -> p d v", d=2)

        def rowb(tb, s, d):
            return tb[:, s, 4 * d:4 * d + 4].rearrange("p (x o) -> p x o", o=1).to_broadcast([P, 4, 64])

        def quad(o_, l, r, *after):
            t = None
            for p in range(2):
                for x in range(4):
                    sl = slice(p * 64, p * 64 + 64)
                    f = mm if x == 3 and p == 1 else mmq
                    t = f(o_[sl, x * 64:x * 64 + 64], l(x, sl), r(x, sl), True, True, *after)
            return t

        def flat3(v):
            return v.rearrange("p x v -> p (x v)")

        ada_jobs = [(I["w_ada"], blk, mods[:, 0, :, :], Q("bada")) for blk in range(4, 12)]
        ada_jobs += [(I[n_], blk, mods[:, 1 + l_, :, :], Q2("bada", l_)) for l_, n_ in enumerate(("w_ada2_0", "w_ada2_1"))
                     for blk in range(12)]
        t_c2 = [t_c]

        def ada_slot():
            if len(ada_jobs) == 24:
                flush()
                t_c2[0] = ada_start(c8(Q2("c", 0)), t_par2, [pe.last(), dve.last()])
            later(ada_block(*ada_jobs.pop(0), t_c2[0]) if ada_jobs else None)

        def chain(d):
            xs = slice(4 * d, 4 * d + 4)
            tA_, tX_, tXt_, tV_, tIT_, tE_, tKt_, tR_, tU_, tT2_, tVb_, tS_, tD_ = (
                b_[:, xs, :] for b_ in (sA, sX, sXt, sV, sIT, sE, sKt, sR, sU, sT2, sVb, sS, sD))

            def half():
                b, ps, free = bank()
                return b, ps[:, 0:256], ps[:, 0:256].rearrange("p (x v) -> p x v", x=4), free

            def comp(tb):
                return lambda x, sl: tb[sl, x, :]

            t_S = t_S0
            t_D = t_A = t_V = t_U = t_T2 = None
            t_IT = t_Kt = t_Vb = t_Xt = None
            for s in range(12):
                n = chunk_of(s, d)
                latent = s >= 4
                kt_, at = (kT, n * 64) if n < 8 else (kTc, (n - 8) * 64)

                def kf(x, sl):
                    return kt_[sl, x, at:at + 64]

                def qf(x, sl):
                    return qT[sl, x, at:at + 64]
                a = tt(dve, tD_, i64b, rowb(Gc, s, d), ALU.mult, t_D)
                bg, pg_, vg, free = half()
                tg = mm(pg_, C("bd"), flat3(tD_), True, True, a, *free)
                bkk, pkk, vkk, free = half()
                tkk = quad(pkk, kf, kf, *free)
                yield
                a1 = tt(dve, tD_, rowb(Gc, s, d), vg, ALU.subtract, tg)
                release(bg, a1)
                a2 = tt(dve, tE_, tD_, mst[:, d:d + 1, :].to_broadcast([P, 4, 64]), ALU.add, a1)
                a3 = af(flat3(tE_), flat3(tE_), ACT.Exp, a2)
                if latent:
                    a5 = tt(dve, tIT_, min_[:, d:d + 1, :].to_broadcast([P, 4, 64]), tD_, ALU.subtract, a1, t_IT)
                    a6 = af(flat3(tIT_), flat3(tIT_), ACT.Exp, a5)
                    t_D = a5
                    bqk, pqk, vqk, free = half()
                    tqk = quad(pqk, kf, qf, *free)
                else:
                    t_D = a2
                a4 = tt(dve, tA_, tE_, vkk, ALU.mult, a3, tkk, t_A)
                release(bkk, a4)
                tA = tt(dve, tA_, tA_, rowb(bet, s, d), ALU.mult, a4)
                tKt = tt(pool, tKt_, ktok[:, n, :, :], rowb(tail, s, d), ALU.mult, t_Kt)
                tVb = tt(pool, tVb_, vtok[:, n, :, :], rowb(bet, s, d), ALU.mult, t_Vb)
                yield
                bv, pv, vv, free = half()
                tv = quad(pv, comp(tA_), lambda x, sl: C("i64")[sl, :], tA, *free)
                if latent:
                    tIT = tt(dve, tIT_, tIT_, vqk, ALU.mult, a6, tqk)
                    release(bqk, tIT)
                a = tt(dve, tV_, vv, lvb(0), ALU.mult, tv)
                release(bv, a)
                tXt = tt(dve, tXt_, i64b, tV_, ALU.subtract, a, t_Xt)
                a = tt(pool, tX_, tA_, lvb(0), ALU.mult, tA)
                tX = tt(pool, tX_, i64b, tX_, ALU.subtract, a)
                yield
                for l in range(1, 6):
                    bv, pv, vv, free = half()
                    tv = quad(pv, comp(tA_), comp(tXt_), tXt, *free)
                    tV = tt(dve, tV_, vv, lvb(l), ALU.mult, tv)
                    release(bv, tV)
                    yield
                    bz, pz, vz, free = half()
                    tz = quad(pz, comp(tX_), comp(tV_), tV, tX, *free)
                    if l < 5:
                        bz2, pz2, vz2, free = half()
                        tz2 = quad(pz2, comp(tV_), comp(tX_), *free)
                    tXt = tt(dve, tXt_, tXt_, vz, ALU.subtract, tz, tv)
                    release(bz, tXt)
                    if l < 5:
                        tX = tt(dve, tX_, tX_, vz2, ALU.subtract, tz2)
                        release(bz2, tX)
                    yield
                t_A = tz
                bs, psS, vS, free = half()
                t = quad(psS, kf, comp(tS_), t_S, *free)
                a = tt(dve, tR_, vS, rowb(beG, s, d), ALU.mult, t)
                release(bs, a)
                t_Vb = tR = tt(dve, tR_, tVb_, tR_, ALU.subtract, a, tVb)
                if latent:
                    bq, pq, vq, free = half()
                    tq = quad(pq, qf, comp(tS_), *free)
                    tT = tt(dve, tT2_, vq, rowb(eG, s, d), ALU.mult, tq, t_T2)
                    release(bq, tT)
                yield
                bu, pu, vu, free = half()
                t_Xt = t = quad(pu, comp(tXt_), comp(tR_), tR, tXt, *free)
                tU = af(flat3(tU_), pu, ACT.Copy, t)
                release(bu, tU)
                a = tt(dve, tS_, tS_, rowb(egl, s, d), ALU.mult, t)
                yield
                bd_, pd, vd, free = half()
                t_Kt = quad(pd, comp(tKt_), comp(tU_), tU, tKt, *free)
                t_S = tt(dve, tS_, tS_, vd, ALU.add, a, t_Kt)
                release(bd_, t_S)
                if latent:
                    bi, pi, vi, free = half()
                    t_IT = quad(pi, comp(tIT_), comp(tU_), tIT, *free)
                    tT = tt(dve, tT2_, tT2_, vi, ALU.add, tT, t_IT)
                    release(bi, tT)
                    dst = oacc[:, n, :, :]
                    if s < 8:
                        t_T2 = copy(pool, dst, tT2_, tT)
                    else:
                        t_T2 = tt(pool, dst, dst, tT2_, ALU.add, tT)
                yield

        t_S0 = t_S
        turns = 0
        chains = [chain(0), chain(1)]
        while chains:
            for c_ in list(chains):
                if next(c_, "end") == "end":
                    chains.remove(c_)
            turns += 1
            if turns % 4 == 0:
                ada_slot()
        while pending or ada_jobs:
            ada_slot()
        gain(A2, 4, 0, Q("gn2"), ada_done[0])
        barrier()
        t_cst2 = d_small[7].start(pool, cst[:, CW - CW2:CW], I["consts2"])

        coming(I["w_1"][4])
        coming(*(I["w_mg"][i] for i in range(8)), cols=384)
        coming(*(I["w_out"][i] for i in range(2)))
        of = oacc.rearrange("p n r v -> p (n r) v")
        o2f = ar[:, 0:2048].rearrange("p (n v) -> p n v", v=64)
        a = tt(dve, o2f, of, of, ALU.mult)
        ssum = mvec[:, 24:56]
        a = rsum(ssum, o2f, a)
        _, a = rsqrt(ssum, ssum, 1.0 / 64, a)
        a = tt(dve, of, of, ssum.rearrange("p (x o) -> p x o", o=1).to_broadcast([P, 32, 64]), ALU.mult, a)
        t_of = a
        act_set(SET_SIGMOID)
        sz = part(10240, 4, T)

        def ev_z(m, j, ps, t, b):
            a = af(sz[:, m, :], ps, ACT.Sigmoid, t)
            a = tt(dve, sz[:, m, :], sz[:, m, :], ps, ALU.mult, a)
            release(b, a)
            split_act(gg[:, 0, m, :], gg[:, 1, m, :], ya[:, m, :], t_of)
        tiles_of(4, [(rh, T)], ev_z)
        yd = part(8192, 4, T)
        for pr in range(4):
            b, ps, free = bank()
            for n in range(8):
                for p in range(2):
                    sl = slice(p * 64, p * 64 + 64)
                    t = mm(ps[sl, n * 64:n * 64 + 64], oacc[sl, n, pr, :], C("i64")[sl, :], True, True, t_of, *free)
            c = stt(yd[:, pr, :], ps, Q("dng"), sz[:, pr, :], ALU.mult, ALU.mult, t)
            release(b, c)
            split_act(gg[:, 0, 4 + pr, :], gg[:, 1, 4 + pr, :], yd[:, pr, :], c)
        slot_done(pe.last())
        t_gg = [act.last(), dve.last()]

        for half in range(2):
            for m in range(4):
                mt = half * 4 + m
                res = []
                for i in range(3):
                    s, hi, lo, t_hi, t_lo = piece()
                    if i < 2:
                        b, ps, free = bank()
                        t = product(ps, lambda k: (hi[:, k, :], lo[:, k, :]), rh, KT, t_hi, t_lo, *free)
                        res.append((b, ps, t))
                    else:
                        pe.wait(*t_gg)
                        for h0 in (0, 4):
                            b, ps, free = bank()
                            t = product(ps, lambda k: (hi[:, h0 + k, :], lo[:, h0 + k, :]),
                                        lambda k: pair(gg, h0 + k), 4, t_hi, t_lo, *free)
                            res.append((b, ps, t))
                    ws_free[s] = t
                (b0, p0, t0), (b1, p1, t1_), (b2, p2, t2), (b3, p3, t3) = res
                u0, u1 = sq[:, 0, :], sq[:, 1, :]
                a = af(u0, p0, ACT.Sigmoid, t0, act.last(), dve.last())
                release(b0, a)
                c = af(u1, p1, ACT.Sigmoid, t1_)
                release(b1, c)
                a = tt(dve, u0, u0, p2, ALU.mult, a, t2)
                release(b2, a)
                c = tt(dve, u1, u1, p3, ALU.mult, c, t3)
                release(b3, c)
                a = tt(dve, u0, u0, u1, ALU.add, a, c)
                split_act(yy[:, 0, mt, :], yy[:, 1, mt, :], u0, a)
        act_set(SET_EXP_LN)
        t_yy = [act.last(), dve.last()]

        def residual(xt, n, part, j, stats=None):
            def ev(base):
                def f(m, jj, ps, t, b):
                    mt = base + m
                    c = stt(xt[:, mt, 0:n], ps[:, 0:n], mod[:, part * 8 + mt, j:j + 1], xt[:, mt, 0:n],
                            ALU.mult, ALU.add, t, dve.last())
                    release(b, c)
                    return stats.tile(xt[:, mt, 0:n], c) if stats else None
                return f
            return ev

        def stats_of(j):
            act.wait(dve.last(), pe.last(), pool.last())
            return Stats((T, TC)[j], [sq[:, i, 0:T] for i in range(2)] if j == 0 else
                         [rs[:, 0:TC], rs[:, TC:T]])

        ry = lambda k: pair(yy, k)
        for half in range(2):
            if half == 0:
                st_x = stats_of(0)
            tiles_of(4, [(ry, T)], residual(xT, T, 2, 0, st_x)(half * 4), pre=t_yy)
        flush()

        def mlp_blocks(w1, w2):
            for q in range(4):
                coming(w1[2 * q], w1[2 * q + 1], w2[2 * q], w2[2 * q + 1])

        def mlp(streams, t_in):
            stats = [None] * len(streams)
            for q in range(4):
                by_k = [[] for _ in streams]

                def ev1(m, j, ps, t, b):
                    hs, hid, xt, n, mj = streams[j]
                    r = sq[:, (m + j) % 2, 0:n]
                    a = af(r, ps[:, 0:n], ACT.Relu, t, dve.last(), pool.last())
                    a2 = tt(dve, r, r, r, ALU.mult, a)
                    release(b, a)
                    by_k[j].append(split_act(hid[:, 0, m, :], hid[:, 1, m, :], r, a2))
                tiles_of(8, [((lambda k, h=st_[0]: pair(h, k)), st_[3]) for st_ in streams], ev1, by_k=t_in)
                if q == 3:
                    stats = [stats_of(st_[4]) for st_ in streams]
                evs = [residual(st_[2], st_[3], 5, st_[4], stats[i])(0) for i, st_ in enumerate(streams)]
                tiles_of(8, [((lambda k, h=st_[1]: pair(h, k)), st_[3]) for st_ in streams],
                         lambda m, j, ps, t, b: evs[j](m, j, ps, t, b), by_k=by_k)
            flush()
            return stats

        def in_blocks(w):
            coming(w[2], w[1])
            coming(w[3], pk=2, pc=512)
            coming(w[0])

        mlp_blocks(I["w_mlp1"], I["w_mlp2"])
        in_blocks(I["w_in2_0"])
        t_n = norm_mod(xT, T, lambda k: col(A2, k), lambda k: mod[:, 24 + k, 0:1], hh, rs[:, :],
                       st_x.root(rs[:, :], pool.last()), ar[:, 8192:9216], dve.last())
        st_m = mlp([(hh, gg, xT, T, 0)], [t_n])
        st_m.append(None)

        t_cx = d_small[3].start(pool, ctx2[:, :, :], I["ctxT2"], pe.last(), dve.last(), act.last())
        for layer in range(2):
            last = layer == 1
            rsc = ar2[:, 11008:11264]
            act.wait(pe.last(), dve.last())
            t_rsc = st_m[1].root(rsc) if st_m[1] else None
            t_rsx = st_m[0].root(rs[:, :])
            barrier()
            mod = mods[:, 1 + layer, :, :]
            A1, A1c, A2, A2c = (mvec[:, 8 * i:8 * i + 8] for i in range(4))
            gain(A1, 1, 0, Q2("gmix", layer), None)
            gain(A1c, 1, 1, Q2("gmix", layer), None)
            gain(A2, 4, 0, Q2("gmlp", layer), None)
            gain(A2c, 4, 1, Q2("gmlp", layer), None)
            lam_init = 0.8 - 0.6 * float(np.exp(-0.3 * layer))
            lv_ = Q2("lam", layer).rearrange("p (i q) -> p i q", i=2)
            l2 = mi[:, 2:4]
            a = tt(dve, l2, lv_[:, :, 0], lv_[:, :, 1], ALU.mult)
            b, ps, free = bank()
            t = mm(ps[:, 0:2], ones[:, :], l2, True, True, a, *free)
            a = af(l2, ps[:, 0:2], ACT.Exp, t)
            release(b, a)
            nlam = mi[:, 4:5]
            a = tt(dve, nlam, mi[:, 3:4], mi[:, 2:3], ALU.subtract, a)
            t_lam = ts(dve, nlam, nlam, -lam_init, None, ALU.add, None, a)
            gs = mi[:, 5:6]
            t_gs = ts(dve, gs, Q2("gsub", layer), 1.0 - lam_init, None, ALU.mult, None)
            barrier()
            t_h = norm_mod(xT, T, lambda k: col(A1, k), lambda k: mod[:, k, 0:1], hh, rs[:, :], t_rsx,
                           ar2[:, 11264:12288])
            if layer == 0:
                t_rsc = rms_rows(ctx2, TC, rsc, t_cx)
            t_hc = norm_mod(ctx2, TC, lambda k: col(A1c, k), lambda k: mod[:, k, 1:2], hc2, rsc, t_rsc,
                            ar2[:, 11264:12288])

            kall = ar2[:, 0:3072].rearrange("p (t n) -> p t n", t=4)
            qc = ar2[:, 3072:4096].rearrange("p (t n) -> p t n", t=4)
            q2 = ar2[:, 4096:6144].rearrange("p (t n) -> p t n", t=4)
            vall = ar2[:, 6144:9216].rearrange("p (t n) -> p t n", t=6)
            rope = ar2[:, 9216:10240].rearrange("p (i n) -> p i n", i=2)
            wpl = ar2[:, 10240:10752].rearrange("p (i n) -> p i n", i=4)
            t_rope = d_small[4].start(pool, rope, I["rope2"], pool.last())
            t_wp = d_small[5].start(pool, wpl, I["w_pool"][layer])
            rc = lambda k: pair(hc2, k)

            def ev_k(m, j, ps, t, b):
                if j == 0:
                    return head_rope(ps, T, None, kall[:, m, 256:768], t, b, True, rope, t_rope, "perm2")
                return head_rope(ps, TC, None, kall[:, m, 0:256], t, b, False, None, None, None)

            def ev_q2(m, j, ps, t, b):
                if j == 0:
                    return head_rope(ps, T, None, q2[:, m, :], t, b, True, rope, t_rope, "perm2")
                return head_rope(ps, TC, None, qc[:, m, :], t, b, False, None, None, None)
            for e in (pe, dve):
                e.wait(t_cst2)
            tiles_of(4, [(rh, T), (rc, TC)], ev_k, by_k=[t_h, t_hc])
            tiles_of(4, [(rh, T)] + ([] if last else [(rc, TC)]), ev_q2)
            flush()
            outs = [bank() for _ in range(6)]
            for kh in range(4):
                s, hi, lo, t_hi, t_lo = piece()
                for i in range(6):
                    b, ps, free = outs[i]
                    src, at = (hc2, i * 128) if i < 2 else (hh, (i - 2) * 128)
                    pe.wait(t_hi, t_lo, *free)
                    for kk in range(2):
                        k = 2 * kh + kk
                        lh, ll = pair(src, k, slice(at, at + 128))
                        for n_, (x_, y_) in enumerate(((lh, hi), (lh, lo), (ll, hi))):
                            f = mm if kk == 1 and n_ == 2 else mmq
                            t = f(ps, x_, y_[:, kk, :], k == 0 and n_ == 0, k == 7 and n_ == 2)
                    if kh == 3:
                        c = af(vall[:, i, :], ps, ACT.Copy, t)
                        release(b, c)
                ws_free[s] = t

            def pool_branch(m, j, ps, t, b):
                n = (T, TC)[j]
                win = (2, 4, 8, 16)[m]
                up = ar2[:, 10752:10752 + n + 32]
                two = (ar2[:, 11296:11296 + n + 32], slot[:, 3072:3072 + n + 32])
                dve.wait(pe.last())
                a = fill(up, 0.0, dve.last(), pe.last())
                for v in two:
                    z = fill(v, 0.0)
                u = af(up[:, 16:16 + n], ps[:, 0:n], ACT.Copy, t, a)
                release(b, u)
                cur, base, w_ = up, u, 1
                while w_ < win:
                    L = n + 32 - w_
                    nxt = two[0] if cur is not two[0] else two[1]
                    base = tt(dve, nxt[:, 0:L], cur[:, 0:L], cur[:, w_:w_ + L], ALU.add, base, z)
                    cur = nxt
                    w_ *= 2
                y = cur[:, 16 - win // 2:16 - win // 2 + n]
                a = ts(dve, y, y, 1.0 / win, None, ALU.mult, None, base)
                ed = C("edge").rearrange("p (g e) -> p g e", g=4)
                a = tt(dve, y[:, 0:8], y[:, 0:8], ed[:, m, 0:8], ALU.mult, a)
                a = tt(dve, y[:, n - 8:n], y[:, n - 8:n], ed[:, m, 8:16], ALU.mult, a)
                a = tt(dve, y, y, up[:, 16:16 + n], ALU.subtract, a)
                yield
                b2, p2, free = bank()
                t = mm(p2[:, 0:n], wpl[:, m, :], y, True, True, a, t_wp, *free)
                dst = mixp[:, m, 0:n] if j == 0 else mixpc[:, m, 0:n]
                c = ts(dve, dst, p2[:, 0:n], Q2("spool", layer)[:, m:m + 1], None, ALU.mult, None, t)
                release(b2, c)

            slot, slot_free, slot_done = reserve()
            mixp = slot[:, 0:2048].rearrange("p (k n) -> p k n", k=4)
            mixpc = slot[:, 2048:3072].rearrange("p (k n) -> p k n", k=4)
            for e in engines:
                e.wait(*slot_free)
            tiles_of(4, [(rh, T)] + ([] if last else [(rc, TC)]), pool_branch)
            barrier()
            for m in range(4):
                split_act(hh[:, 0, m, :], hh[:, 1, m, :], mixp[:, m, :])
                if not last:
                    split_act(hc2[:, 0, m, :], hc2[:, 1, m, :], mixpc[:, m, :])
            slot_done(*barrier())
            wo = I[("w_out2_0", "w_out2_1")[layer]]
            coming(wo[0], wo[1])
            mlp_blocks(I[("w_m1_0", "w_m1_1")[layer]], I[("w_m2_0", "w_m2_1")[layer]])
            if not last:
                in_blocks(I["w_in2_1"])

            jobs2 = [(0, qb, t4) for qb in range(4) for t4 in range(4)]
            if not last:
                jobs2 += [(1, qb, t4) for qb in range(2) for t4 in range(4)]
            e_buf = [ar2[:, 9216 + i * 768:9216 + (i + 1) * 768] for i in range(2)]
            e_second = ar2[:, 11520:12288]
            p_t = ar2[:, 10752:10752 + 768].rearrange("p (j q) -> p j q", j=6)
            held_out = {}
            rotating[0] = 6
            st2 = {}

            def scores2(i):
                kind, qb, t4 = jobs2[i]
                n = TC if kind else 768
                qsrc = qc if kind else q2
                got = []
                for p in range(2):
                    sl = slice(p * 64, p * 64 + 64)
                    b, ps, free = bank2()
                    q = qsrc[sl, t4, qb * 128:qb * 128 + 128]
                    for a0 in range(0, n, 512):
                        a1 = min(n, a0 + 512)
                        t = mm(ps[:, a0:a1], q, kall[sl, t4, a0:a1], True, True, *free)
                    got.append((b, ps, t))
                st2[i] = (n, got)

            e_free = [None, None]
            e_done = [None]
            pt2_free = [None]
            vb_free = [None, None]

            def soft2(i):
                n, got = st2[i]
                sm = mvec[:, 40 + (i % 2) * 8:48 + (i % 2) * 8]
                ends = []
                e0, e1 = e_buf[i % 2][:, 0:n], e_second[:, 0:n]
                for p, (b, ps, t) in enumerate(got):
                    nm, su = sm[:, 2 * p:2 * p + 1], sm[:, 2 * p + 1:2 * p + 2]
                    a = rmax(nm, ps[:, 0:n], t)
                    a = ts(dve, nm, nm, -0.125, None, ALU.mult, None, a)
                    a = af((e0, e1)[p], ps[:, 0:n], ACT.Exp, a, e_free[i % 2], e_done[0], scale=0.125, bias=nm, accum=su)
                    release2(b, a)
                    ends.append(a)
                yield
                a = recip(sm[:, 1:4:2], sm[:, 1:4:2], *ends)
                r1 = sm[:, 3:4]
                a = tt(dve, r1, r1, nlam, ALU.mult, a)
                c = ts(dve, e1, e1, r1, None, ALU.mult, None, a)
                e_done[0] = c = stt(e0, e0, sm[:, 1:2], e1, ALU.mult, ALU.add, c)
                st2[i] = (n, c)

            def out2(i):
                kind, qb, t4 = jobs2[i]
                n, c = st2.pop(i)
                nt = n // 128
                b, ps, free = bank2()
                for j in range(nt):
                    t = flip(ps[:, j * 128:j * 128 + 128], e_buf[i % 2][:, j * 128:j * 128 + 128], c, *free)
                e_free[i % 2] = t
                c = af(p_t[:, 0:nt, :].rearrange("p j q -> p (j q)"), ps[:, 0:n], ACT.Copy, t, pt2_free[0])
                release2(b, c)
                yield
                if t4 == 0:
                    held_out[(kind, qb)] = bank_held()
                ob, po_, free = held_out[(kind, qb)]
                for j in range(nt):
                    t = mm(po_[:, t4 * 128:t4 * 128 + 128], vall[:, j, t4 * 128:t4 * 128 + 128], p_t[:, j, :],
                           j == 0, j == nt - 1, c, *free)
                pt2_free[0] = t
                if tail:
                    tail.pop()(b, ps)
                if t4 == 3:
                    s0 = sq[:, 0, :]
                    a = af(s0, po_, ACT.Square, t, dve.last(), act.last())

                    def finish(b1, p1):
                        m_ = mm(p1[:, 0:512], ones[:, :], s0, True, True, a, *bank_free[b1])
                        r = sq[:, 1, :]
                        a0, a1 = rsqrt(r, p1[:, 0:512], 1.0 / 128, m_, dve.last())
                        release2(b1, a0)
                        c_ = stt(s0, po_, gs, r, ALU.mult, ALU.mult, a1)
                        release(ob, c_)
                        dst = hc2 if kind else hh
                        sv = s0.rearrange("p (t q) -> p t q", t=4)
                        split_act(dst[:, 0, 4:8, qb * 128:qb * 128 + 128], dst[:, 1, 4:8, qb * 128:qb * 128 + 128],
                                  sv, c_)
                    tail.append(finish)
                    if i == len(jobs2) - 1:
                        tail.pop()(b, ps)
                yield

            tail = []
            scores2(0)
            for i in range(len(jobs2)):
                soft, outs_ = soft2(i), out2(i - 1) if i else iter(())
                next(soft)
                next(outs_, None)
                next(soft, None)
                if i + 1 < len(jobs2):
                    scores2(i + 1)
                next(outs_, None)
            for _ in out2(len(jobs2) - 1):
                pass
            rotating[0] = 8
            pre = barrier()
            streams = [(rh, T)] + ([] if last else [(rc, TC)])
            for half in range(2):
                if half == 0:
                    st_x = stats_of(0)
                    st_c = None if last else stats_of(1)
                evs = [residual(xT, T, 2, 0, st_x)(half * 4), residual(ctx2, TC, 2, 1, st_c)(half * 4)]
                tiles_of(4, streams, lambda m, j, ps, t, b: evs[j](m, j, ps, t, b))
            flush()
            act.wait(pe.last(), dve.last())
            rsc = ar2[:, 11008:11264]
            t_rsc = None if last else st_c.root(rsc)
            t_n = [norm_mod(xT, T, lambda k: col(A2, k), lambda k: mod[:, 24 + k, 0:1], hh, rs[:, :],
                            st_x.root(rs[:, :]), ar2[:, 9216:10240])]
            if not last:
                t_n.append(norm_mod(ctx2, TC, lambda k: col(A2c, k), lambda k: mod[:, 24 + k, 1:2], hc2, rsc, t_rsc,
                                    ar2[:, 9216:10240]))
            st_list = [(hh, g2, xT, T, 0)] + ([] if last else [(hc2, gc2, ctx2, TC, 1)])
            st_m = mlp(st_list, t_n)

        t_rs = st_m[0].root(rs[:, :], pool.last())
        for k in range(KT):
            a = stt(xT[:, k, :], xT[:, k, :], Q2("gfin", 0)[:, k:k + 1], rs[:, :], ALU.mult, ALU.mult, t_rs)
        d_out = Dma(sem("d_out"), "d_out")
        t = d_out.start(sp, out, xT[:, :, :], a)
        sp.wait(t)

        with nc.Block() as block:
            @block.tensor
            def _(e):
                for f in pe.ops:
                    f(e)

            @block.vector
            def _(e):
                for f in dve.ops:
                    f(e)

            @block.scalar
            def _(e):
                for f in act.ops:
                    f(e)

            @block.gpsimd
            def _(e):
                for f in pool.ops:
                    f(e)

            @block.sync
            def _(e):
                for f in sp.ops:
                    f(e)


def constants():
    c = {}
    i, j = np.arange(P)[:, None], np.arange(P)[None, :]
    same = i // 64 == j // 64
    c["ident"] = i == j
    c["bd"] = same
    for name, h in (("perm1", 16), ("perm2", 32)):
        c[name] = np.where((j % (2 * h) < h) & (i == j + h), -1.0, 0.0) + ((j % (2 * h) >= h) & (i == j - h))
    c["trif"] = same & (i <= j)
    c["trib"] = same & (i >= j)
    c["mprev"] = np.where(j >= i, 0.0, NEG)
    c["mnext"] = np.where(j <= i, 0.0, NEG)
    r, v = np.arange(P)[:, None] % 64, np.arange(64)[None, :]
    c["i64"] = r == v
    c["mstrict"] = np.concatenate([np.where(r > v, 0.0, NEG), np.where(r < v, 0.0, NEG)], 1)
    c["mincl"] = np.concatenate([np.where(v >= r, 0.0, NEG), np.where(v <= r, 0.0, NEG)], 1)
    c["lvl"] = np.concatenate([(r // (2 * s) == v // (2 * s)) & (r // s != v // s) for s in (1, 2, 4, 8, 16, 32)], 1)
    sel = np.zeros((P, 2, 2, 2, 4))
    for p in range(2):
        for d in range(2):
            for pr in range(4):
                for b in range(2):
                    sel[32 * b + 8 * d + 2 * pr + p, p, b, d, pr] = 1.0
    c["sel"] = sel.reshape(P, 32)
    edge = np.ones((4, 16))
    for g, w in enumerate((2, 4, 8, 16)):
        for t in range(8):
            edge[g, t] = w / min(w, t + w // 2)
            edge[g, 15 - t] = w / min(w, t + 1 + w // 2)
    c["edge"] = np.broadcast_to(edge.reshape(1, 64), (P, 64))
    small = np.concatenate([np.asarray(c[n], np.float32) for n, _ in CONSTS], 1)
    assert small.shape == (P, CW)
    t = np.arange(T)
    freqs = (10000.0 ** (-np.arange(16) / 16.0)).astype(np.float32).astype(np.float64)
    row, column = t // 64, t % 64
    m = np.arange(64)
    ang1 = np.where((m < 32)[:, None], row[None, :], column[None, :]) * freqs[m % 16][:, None]
    ang2 = np.where((m % 32 < 16)[:, None], row[None, :], column[None, :]) * freqs[m % 16][:, None]
    ropes = [np.stack([np.cos(np.tile(a, (2, 1))), np.sin(np.tile(a, (2, 1)))], 1).astype(np.float32)
             for a in (ang1, ang2)]
    return small, np.concatenate([np.asarray(c[n], np.float32) for n, _ in CONSTS2], 1), ropes[0], ropes[1]


def kernel(**inputs):
    import concourse.bacc as bacc
    from concourse.bass_utils import run_bass_kernel_spmd

    x = {k: np.asarray(v) for k, v in inputs.items()}

    def tiles(w, cols=512):
        k, n = w.shape
        return np.ascontiguousarray(w.reshape(k // P, P, n // cols, cols).transpose(2, 1, 0, 3)).reshape(
            n // cols, P, -1)

    def fm(a):
        return np.ascontiguousarray(a.T.reshape(KT, P, -1).transpose(1, 0, 2))

    def vec(v):
        return v.reshape(-1, P).T

    A = {}
    A["consts"], A["consts2"], A["rope1"], A["rope2"] = constants()
    A["xT"], A["ctxT"], A["ctxT2"] = fm(x["x"][0]), fm(x["ctx"][0]), fm(x["ctx_2"][0])
    w = x["w_in"][0]
    cut = np.cumsum([0, 512, 128, 128, 512, 512, 512, 512, 16, 16, 1024, 1024])
    aq, ak, av, dq, dk, dv, dz, da, db, ga, gd = (w[:, a:b] for a, b in zip(cut[:-1], cut[1:]))
    order = np.array([0, 4, 1, 5, 2, 6, 3, 7])
    aq = aq.reshape(1024, 8, 64)[:, order].reshape(1024, 512)
    A["w_kv"] = tiles(np.concatenate([ak, av], 1), 256)[0]
    A["w_ab"] = tiles(np.concatenate([da, np.zeros((1024, 16), w.dtype), db], 1), 48)[0]
    A["w_1"] = np.concatenate([tiles(m) for m in (aq, dk, dv, dq, dz)], 0)
    br = np.concatenate([x["w_br_attn"][0].reshape(8, 64, 1024)[order].reshape(512, 1024), x["w_br_dn"][0]], 0)
    A["w_mg"] = np.concatenate([tiles(np.concatenate([m[:, i * P:i * P + P] for m in (ga, gd, br)], 1), 384)
                                for i in range(8)], 0)
    A["w_out"] = tiles(x["w_out"][0])
    A["w_ada"] = tiles(x["w_ada"][0])

    def mlp_tiles(w1, w2):
        return tiles(w1), np.concatenate([tiles(w2[q * 1024:(q + 1) * 1024]) for q in range(4)], 0)

    A["w_mlp1"], A["w_mlp2"] = mlp_tiles(x["w_mlp1"][0], x["w_mlp2"][0])

    def rows(v, at=0):
        out = np.zeros((P, 1), v.dtype)
        out[at:at + v.size, 0] = v
        return out

    def cvecs(c, cc):
        return np.stack([vec(c), vec(cc)], 2).reshape(P, 16)

    A["par1"] = np.concatenate([
        cvecs(x["c"][0], x["c_ctx"]), vec(x["b_ada"][0]), vec(x["g_norm1"][0]), vec(x["g_norm2"][0]),
        np.tile(x["q_norm_g"][0], 2)[:, None], np.tile(x["k_norm_g"][0], 2)[:, None],
        np.broadcast_to(x["attn_sink"][0][None], (P, 8)),
        np.concatenate([vec(x["conv_w"][0][t]) for t in range(3)], 1),
        rows(x["a_log"][0].reshape(-1)), rows(x["dt_bias"][0].reshape(-1)),
        np.tile(x["dn_norm_g"][0], 2)[:, None]], 1)
    par2, pools = [], []
    for l in range(2):
        lam = np.concatenate([rows(x[n][l]) for n in ("lam_q1_2", "lam_k1_2", "lam_q2_2", "lam_k2_2")], 1)
        par2.append(np.concatenate([
            cvecs(x["c_2"][0], x["c_ctx_2"]), vec(x["b_ada_2"][l]), vec(x["g_mix_2"][l]), vec(x["g_mlp_2"][l]),
            vec(x["s_pool_2"][l]), x["g_subln_2"][l][:, None], lam,
            vec(x["g_final_2"])], 1))
        A[f"w_ada2_{l}"] = tiles(x["w_ada_2"][l])
        A[f"w_in2_{l}"] = tiles(x["w_in_2"][l])
        A[f"w_out2_{l}"] = tiles(x["w_out_2"][l])
        A[f"w_m1_{l}"], A[f"w_m2_{l}"] = mlp_tiles(x["w_mlp1_2"][l], x["w_mlp2_2"][l])
    A["par2"] = np.stack(par2, 1)
    A["w_pool"] = np.ascontiguousarray(x["w_pool_2"].transpose(0, 2, 1, 3))

    nc = bacc.Bacc("TRN2", target_bir_lowering=False, num_devices=1)
    arrays, I = {}, {}
    for name, a in A.items():
        a = np.ascontiguousarray(a)
        arrays[f"in_{name}"] = a
        I[name] = nc.dram_tensor(f"in_{name}", a.shape, F32, kind="ExternalInput").ap()
    out = nc.dram_tensor("out_x", (P, KT, T), F32, kind="ExternalOutput").ap()
    build(nc, I, out)
    got = run_bass_kernel_spmd(nc, [arrays], core_ids=[0]).results[0]["out_x"]
    return np.ascontiguousarray(got.transpose(2, 1, 0)).reshape(1, T, 1024)
```
